# Optimizing a Trainium2 kernel written in Bass

```python
import jax
import jax.numpy as jnp
from jax import lax
import numpy as np

D_MODEL = 1024
BATCH = 1
SEQ = 256
DEPTH = 2

HEAD_DIM = 64
SWA_Q_HEADS = 8
SWA_KV_HEADS = 2
SWA_WINDOW = 128
SWA_BLOCK = 128
MOBA_HEADS = 8
MOBA_BLOCK = 256
MOBA_TOPK = 3
MOBA_Q_CHUNK = 128
GLA_HEADS = 4
GLA_DK = 64
GLA_DV = 128
GLA_GATE_RANK = 16
GLA_GATE_TEMP = 16.0
GLA_CHUNK = 64
N_BRANCH = 3
SWA_OUT_W = SWA_Q_HEADS * HEAD_DIM
MOBA_OUT_W = MOBA_HEADS * HEAD_DIM
GLA_OUT_W = GLA_HEADS * GLA_DV
D_FF = 2816
N_EXPERTS = 8
TOP_K = 2
D_FF_EXPERT = 1408
RMS_EPS = 1e-6
N_DENSE = (DEPTH + 1) // 2
N_MOE = DEPTH // 2
IN_WIDTHS = (SWA_Q_HEADS * HEAD_DIM, SWA_KV_HEADS * HEAD_DIM, SWA_KV_HEADS * HEAD_DIM,
             MOBA_HEADS * HEAD_DIM, MOBA_HEADS * HEAD_DIM, MOBA_HEADS * HEAD_DIM,
             GLA_HEADS * GLA_DK, GLA_HEADS * GLA_DK, GLA_HEADS * GLA_DV, GLA_HEADS * GLA_DV,
             GLA_GATE_RANK, N_BRANCH * D_MODEL)
IN_TOTAL = sum(IN_WIDTHS)

kernel_name = 'hybrid_swa_moba_gla_moe_block'

def rms_norm(x, g):
    xf = x.astype(jnp.float32)
    y = xf * lax.rsqrt(jnp.mean(xf * xf, axis=-1, keepdims=True) + RMS_EPS)
    return (y * g.astype(jnp.float32)).astype(x.dtype)

def swa_sink_attention(q, k, v, sinks):
    B, S, _, dh = q.shape
    nb = S // SWA_BLOCK
    G = SWA_Q_HEADS // SWA_KV_HEADS
    qb = q.reshape(B, nb, SWA_BLOCK, SWA_KV_HEADS, G, dh)
    kb = k.reshape(B, nb, SWA_BLOCK, SWA_KV_HEADS, dh)
    vb = v.reshape(B, nb, SWA_BLOCK, SWA_KV_HEADS, dh)
    zk = jnp.zeros_like(kb[:, :1])
    k2 = jnp.concatenate([jnp.concatenate([zk, kb[:, :-1]], axis=1), kb], axis=2)
    v2 = jnp.concatenate([jnp.concatenate([zk, vb[:, :-1]], axis=1), vb], axis=2)
    s = jnp.einsum('bnqhgd,bnkhd->bnhgqk', qb, k2).astype(jnp.float32) * (dh ** -0.5)
    qi = jnp.arange(SWA_BLOCK)[:, None]
    kj = jnp.arange(2 * SWA_BLOCK)[None, :]
    rel = qi + SWA_BLOCK - kj
    band = (rel >= 0) & (rel < SWA_WINDOW)
    blk = jnp.arange(nb)[:, None, None]
    mask = band[None] & ((blk > 0) | (kj >= SWA_BLOCK)[None])
    s = jnp.where(mask[None, :, None, None], s, -jnp.inf)
    sink = sinks.astype(jnp.float32).reshape(SWA_KV_HEADS, G)[None, None, :, :, None, None]
    sink = jnp.broadcast_to(sink, s.shape[:-1] + (1,))
    p = jax.nn.softmax(jnp.concatenate([s, sink], axis=-1), axis=-1)[..., :-1]
    o = jnp.einsum('bnhgqk,bnkhd->bnqhgd', p.astype(v.dtype), v2)
    return o.reshape(B, S, SWA_Q_HEADS * dh)

def moba_attention(q, k, v):
    B, S, H, dh = q.shape
    nblk = -(-S // MOBA_BLOCK)
    s_pad = nblk * MOBA_BLOCK
    padw = ((0, 0), (0, s_pad - S), (0, 0), (0, 0))
    kb = jnp.pad(k, padw).reshape(B, nblk, MOBA_BLOCK, H, dh).transpose(0, 3, 1, 2, 4)
    vb = jnp.pad(v, padw).reshape(B, nblk, MOBA_BLOCK, H, dh).transpose(0, 3, 1, 2, 4)
    kbar = jnp.mean(kb.astype(jnp.float32), axis=3).astype(q.dtype)
    qh = q.transpose(0, 2, 1, 3)
    topk = min(MOBA_TOPK, nblk)
    nq = S // MOBA_Q_CHUNK
    scale = dh ** -0.5
    bidx = jnp.arange(B)[:, None, None, None]
    hidx = jnp.arange(H)[None, :, None, None]
    blk_ids = jnp.arange(nblk)

    def chunk(ci):
        start = ci * MOBA_Q_CHUNK
        qc = lax.dynamic_slice_in_dim(qh, start, MOBA_Q_CHUNK, axis=2)
        cur = start // MOBA_BLOCK
        qpos = start + jnp.arange(MOBA_Q_CHUNK)
        gs = jnp.einsum('bhqd,bhnd->bhqn', qc, kbar).astype(jnp.float32)
        gs = jnp.where(blk_ids < cur, gs, -jnp.inf)
        _, idx = lax.top_k(gs, topk)
        valid = jnp.arange(topk) < cur
        kg = kb[bidx, hidx, idx]
        vg = vb[bidx, hidx, idx]
        s_sel = jnp.einsum('bhqd,bhqrkd->bhqrk', qc, kg).astype(jnp.float32) * scale
        s_sel = jnp.where(valid[:, None], s_sel, -jnp.inf).reshape(B, H, MOBA_Q_CHUNK, topk * MOBA_BLOCK)
        ko = lax.dynamic_index_in_dim(kb, cur, axis=2, keepdims=False)
        vo = lax.dynamic_index_in_dim(vb, cur, axis=2, keepdims=False)
        kpos = cur * MOBA_BLOCK + jnp.arange(MOBA_BLOCK)
        s_own = jnp.einsum('bhqd,bhkd->bhqk', qc, ko).astype(jnp.float32) * scale
        s_own = jnp.where(kpos[None, :] <= qpos[:, None], s_own, -jnp.inf)
        p = jax.nn.softmax(jnp.concatenate([s_sel, s_own], axis=-1), axis=-1).astype(v.dtype)
        p_sel = p[..., :topk * MOBA_BLOCK].reshape(B, H, MOBA_Q_CHUNK, topk, MOBA_BLOCK)
        p_own = p[..., topk * MOBA_BLOCK:]
        return (jnp.einsum('bhqrk,bhqrkd->bhqd', p_sel, vg)
                + jnp.einsum('bhqk,bhkd->bhqd', p_own, vo))

    out = lax.map(chunk, jnp.arange(nq))
    return out.transpose(1, 0, 3, 2, 4).reshape(B, S, H * dh)

def gla_attention(q, k, v, g_log):
    B, S, H, dk = q.shape
    dv = v.shape[-1]
    C = GLA_CHUNK
    nc = S // C

    def to_chunks(t):
        return t.astype(jnp.float32).reshape(B, nc, C, H, t.shape[-1]).transpose(0, 3, 1, 2, 4)

    qc = to_chunks(q) * (dk ** -0.5)
    kc = to_chunks(k)
    vc = to_chunks(v)
    b = jnp.cumsum(to_chunks(g_log), axis=3)
    b_last = b[:, :, :, -1:, :]
    q_in = qc * jnp.exp(b)
    k_in = kc * jnp.exp(-b)
    causal = jnp.tril(jnp.ones((C, C), dtype=bool))
    a = jnp.where(causal, jnp.einsum('bhntd,bhnsd->bhnts', q_in, k_in), 0.0)
    o_intra = jnp.einsum('bhnts,bhnse->bhnte', a, vc)
    u = jnp.einsum('bhnsd,bhnse->bhnde', kc * jnp.exp(b_last - b), vc)
    decay = jnp.exp(b_last[:, :, :, 0, :])

    def step(state, xs):
        u_n, d_n = xs
        return d_n[..., None] * state + u_n, state

    _, s_prev = lax.scan(step, jnp.zeros((B, H, dk, dv), jnp.float32),
                         (u.transpose(2, 0, 1, 3, 4), decay.transpose(2, 0, 1, 3)))
    s_prev = s_prev.transpose(1, 2, 0, 3, 4)
    o = o_intra + jnp.einsum('bhntd,bhnde->bhnte', q_in, s_prev)
    return o.transpose(0, 2, 3, 1, 4).reshape(B, S, H, dv)

def mixer_block(h, w_in, sinks, gla_w_gate, gla_b_gate, gla_norm_g, w_branch_a, w_branch_b, w_branch_c, w_o):
    B, S, _ = h.shape
    split_idx = [int(c) for c in np.cumsum(IN_WIDTHS)[:-1]]
    (a_q, a_k, a_v, b_q, b_k, b_v, c_q, c_k, c_v, c_r, c_g, gates) = jnp.split(h @ w_in, split_idx, axis=-1)
    o_a = swa_sink_attention(a_q.reshape(B, S, SWA_Q_HEADS, HEAD_DIM),
                             a_k.reshape(B, S, SWA_KV_HEADS, HEAD_DIM),
                             a_v.reshape(B, S, SWA_KV_HEADS, HEAD_DIM), sinks)
    o_b = moba_attention(b_q.reshape(B, S, MOBA_HEADS, HEAD_DIM),
                         b_k.reshape(B, S, MOBA_HEADS, HEAD_DIM),
                         b_v.reshape(B, S, MOBA_HEADS, HEAD_DIM))
    g_log = jax.nn.log_sigmoid((c_g @ gla_w_gate + gla_b_gate).astype(jnp.float32)) / GLA_GATE_TEMP
    o_c = gla_attention(c_q.reshape(B, S, GLA_HEADS, GLA_DK), c_k.reshape(B, S, GLA_HEADS, GLA_DK),
                        c_v.reshape(B, S, GLA_HEADS, GLA_DV), g_log.reshape(B, S, GLA_HEADS, GLA_DK))
    o_c = o_c * lax.rsqrt(jnp.mean(o_c * o_c, axis=-1, keepdims=True) + RMS_EPS)
    o_c = o_c * gla_norm_g.astype(jnp.float32).reshape(GLA_HEADS, GLA_DV)
    o_c = (o_c.reshape(B, S, GLA_OUT_W) * jax.nn.silu(c_r.astype(jnp.float32))).astype(h.dtype)
    g = jax.nn.sigmoid(gates).reshape(B, S, N_BRANCH, D_MODEL)
    y = g[:, :, 0] * (o_a @ w_branch_a) + g[:, :, 1] * (o_b @ w_branch_b) + g[:, :, 2] * (o_c @ w_branch_c)
    return y @ w_o

def swiglu(h, w_gate, w_up, w_down):
    return (jax.nn.silu(h @ w_gate) * (h @ w_up)) @ w_down

def moe_swiglu(h, w_router, w_gate, w_up, w_down):
    B, S, D = h.shape
    t = h.reshape(B * S, D)
    logits = (t @ w_router).astype(jnp.float32)
    top_v, top_i = lax.top_k(logits, TOP_K)
    top_p = jax.nn.softmax(top_v, axis=-1)
    combine = jnp.sum(jax.nn.one_hot(top_i, N_EXPERTS, dtype=jnp.float32) * top_p[..., None], axis=1)
    out = jnp.zeros_like(t)
    for e in range(N_EXPERTS):
        out = out + combine[:, e:e + 1].astype(t.dtype) * swiglu(t, w_gate[e], w_up[e], w_down[e])
    return out.reshape(B, S, D)

def setup_inputs(seed: int = 0) -> dict:
    key = jax.random.key(seed)
    ks = jax.random.split(key, 20)
    f32 = jnp.float32

    def nrm(k, shape, scale):
        return jax.random.normal(k, shape, f32) * scale

    def gain(k, shape):
        return 1.0 + 0.02 * jax.random.normal(k, shape, f32)

    return {
        'x': nrm(ks[0], (BATCH, SEQ, D_MODEL), 1.0),
        'norm1_g': gain(ks[1], (DEPTH, D_MODEL)),
        'w_in': nrm(ks[2], (DEPTH, D_MODEL, IN_TOTAL), D_MODEL ** -0.5),
        'swa_sinks': nrm(ks[3], (DEPTH, SWA_Q_HEADS), 0.5),
        'gla_w_gate': nrm(ks[4], (DEPTH, GLA_GATE_RANK, GLA_HEADS * GLA_DK), GLA_GATE_RANK ** -0.5),
        'gla_b_gate': nrm(ks[5], (DEPTH, GLA_HEADS * GLA_DK), 0.1),
        'gla_norm_g': gain(ks[6], (DEPTH, GLA_OUT_W)),
        'w_branch_a': nrm(ks[7], (DEPTH, SWA_OUT_W, D_MODEL), SWA_OUT_W ** -0.5),
        'w_branch_b': nrm(ks[8], (DEPTH, MOBA_OUT_W, D_MODEL), MOBA_OUT_W ** -0.5),
        'w_branch_c': nrm(ks[9], (DEPTH, GLA_OUT_W, D_MODEL), GLA_OUT_W ** -0.5),
        'w_o': nrm(ks[10], (DEPTH, D_MODEL, D_MODEL), D_MODEL ** -0.5),
        'norm2_g': gain(ks[11], (DEPTH, D_MODEL)),
        'ffn_w_gate': nrm(ks[12], (N_DENSE, D_MODEL, D_FF), D_MODEL ** -0.5),
        'ffn_w_up': nrm(ks[13], (N_DENSE, D_MODEL, D_FF), D_MODEL ** -0.5),
        'ffn_w_down': nrm(ks[14], (N_DENSE, D_FF, D_MODEL), D_FF ** -0.5),
        'moe_router': nrm(ks[15], (N_MOE, D_MODEL, N_EXPERTS), D_MODEL ** -0.5),
        'moe_w_gate': nrm(ks[16], (N_MOE, N_EXPERTS, D_MODEL, D_FF_EXPERT), D_MODEL ** -0.5),
        'moe_w_up': nrm(ks[17], (N_MOE, N_EXPERTS, D_MODEL, D_FF_EXPERT), D_MODEL ** -0.5),
        'moe_w_down': nrm(ks[18], (N_MOE, N_EXPERTS, D_FF_EXPERT, D_MODEL), D_FF_EXPERT ** -0.5),
        'final_norm_g': gain(ks[19], (D_MODEL,)),
    }

def reference(x, norm1_g, w_in, swa_sinks, gla_w_gate, gla_b_gate, gla_norm_g, w_branch_a, w_branch_b,
              w_branch_c, w_o, norm2_g, ffn_w_gate, ffn_w_up, ffn_w_down, moe_router, moe_w_gate, moe_w_up,
              moe_w_down, final_norm_g):
    for l in range(DEPTH):
        h = rms_norm(x, norm1_g[l])
        x = x + mixer_block(h, w_in[l], swa_sinks[l], gla_w_gate[l], gla_b_gate[l], gla_norm_g[l],
                            w_branch_a[l], w_branch_b[l], w_branch_c[l], w_o[l])
        h = rms_norm(x, norm2_g[l])
        j = l // 2
        if l % 2 == 0:
            x = x + swiglu(h, ffn_w_gate[j], ffn_w_up[j], ffn_w_down[j])
        else:
            x = x + moe_swiglu(h, moe_router[j], moe_w_gate[j], moe_w_up[j], moe_w_down[j])
    return rms_norm(x, final_norm_g)


_drawn_inputs = setup_inputs


def setup_inputs(seed=0):
    import zlib

    import numpy as np

    out = dict(_drawn_inputs(seed))
    spreads = {}
    factors = {}
    for name, (base, spread) in spreads.items():
        noise = np.random.default_rng([zlib.crc32(name.encode()), seed]).standard_normal(out[name].shape)
        drawn = base * np.exp(spread * noise) if base else spread * noise
        out[name] = jnp.asarray(drawn.astype(out[name].dtype))
    for name, factor in factors.items():
        out[name] = (out[name] * factor).astype(out[name].dtype)
    return out
```

```python
from contextlib import ExitStack

import concourse.bass as bass
from concourse import mybir

F32 = mybir.dt.float32
F32R = mybir.dt.float32r
U32 = mybir.dt.uint32
I32 = mybir.dt.int32
ALU = mybir.AluOpType
ACT = mybir.ActivationFunctionType
AX = mybir.AxisListType

P = 128
T, D, LAYERS = 256, 1024, 2
TT = T // P
KD = D // P
DH = 64
SWA_H, SWA_KV, MOBA_H = 8, 2, 8
GH, GDK, GDV, GRANK, CH = 4, 64, 128, 16, 64
BW = 512
F, FE, NE = 2816, 1408, 8
EPS = 1e-6
NEG = -1.0e30

A0, B0, C0, G0 = 0, 768, 2304, 3856
SW = 386
SLABS = {
    "C4": (3840, SW, [("g", 0, 1, "cg", 0), ("t", 0, 16, 370), ("t", 1, 16, 370)]),
    "C0": (C0, 384, [("f", 0, 2, "cq", 0), ("f", 2, 1, "ck", 0)]),
    "C1": (C0 + 384, 384, [("f", 0, 1, "ck", 1), ("t", 0, 128, 256), ("t", 1, 128, 256)]),
    "C2": (C0 + 768, 384, [("t", 0, 0, 384), ("t", 1, 0, 384)]),
    "C3": (C0 + 1152, 384, [("t", 0, 0, 384), ("t", 1, 0, 384)]),
    "A0": (A0, 384, [("f", 0, 2, "aq", 0), ("f", 2, 1, "aq", 2)]),
    "A1": (A0 + 384, 384, [("f", 0, 1, "aq", 3), ("f", 1, 1, "ak", 0), ("t", 0, 256, 128), ("t", 1, 256, 128)]),
    "B0": (B0, 384, [("f", 0, 2, "bq", 0), ("f", 2, 1, "bq", 2)]),
    "B1": (B0 + 384, 384, [("f", 0, 1, "bq", 3), ("f", 1, 2, "bk", 0)]),
    "B2": (B0 + 768, 384, [("f", 0, 2, "bk", 2), ("t", 0, 256, 128), ("t", 1, 256, 128)]),
    "B3": (B0 + 1152, 384, [("t", 0, 0, 384), ("t", 1, 0, 384)]),
}
for _g in range(1, 8):
    SLABS[f"G{_g}"] = (3840 + SW * _g, SW, [("t", 0, 0, SW), ("t", 1, 0, SW)])
GATE0 = SW - GRANK

PIECES = {
    "C4": [(0, GATE0, "gates", 0)],
    "C1": [(0, 256, "cv", 0)],
    "C2": [(0, 256, "cv", 256), (256, 128, "cr", 0)],
    "C3": [(0, 384, "cr", 128)],
    "A1": [(0, 128, "av", 0)],
    "B2": [(0, 128, "bv", 0)],
    "B3": [(0, 384, "bv", 128)],
}
for _g in range(1, 8):
    PIECES[f"G{_g}"] = [(0, SW, "gates", GATE0 + SW * (_g - 1))]

WCOLS = [(0, 352), (352, 352), (704, 320)]
FC = 352
NF, NFE = F // FC, FE // FC
FT, FET = F // P, FE // P
DK = 3
HALF = D // 2


def blocks_done(c):
    return (c + 1) * FC // P


def down_groups(tiles):
    return [(k, min(DK, tiles - k)) for k in range(0, tiles, DK)]


def block_pairs(c):
    a, b = (blocks_done(c - 1) if c else 0), blocks_done(c)
    return [(j, min(2, b - j)) for j in range(a, b, 2)]


def mixer_steps():
    names = ["norm", "C4", "C0", "z", "C1", "bT", "C2", "C3", "kdT", "aT", "A0", "u", "A1", "swap", "oC",
             "S0", "B0", "P0", "S1", "B1", "V0", "P1", "oCT", "B2", "V1", "B3",
             "S2", "G1", "P2", "S3", "G2", "V2", "P3", "G3", "V3", "G4", "G5", "G6", "G7"]
    out = [(n, 0) for n in names]
    out += [("branch", 3 * b + s) for b in range(3) for s in range(3)]
    return out + [("yT", 0)] + [("wo", s) for s in range(3)] + [("norm2", 0)]


def dense_steps():
    out = []
    for c in range(NF):
        out += [("gate", c), ("up", c)]
        if c:
            out.append(("hT", c - 1))
    for g in range(len(down_groups(FT))):
        if g == 3:
            out.append(("hT", NF - 1))
        out.append(("down", g))
    return out


STEPS = {l: mixer_steps() + (dense_steps() if l == 0 else []) for l in range(LAYERS)}


def sizes(step):
    name, i = step
    if name in SLABS:
        return 2, len(SLABS[name][2]), 0, 0
    if name in ("norm", "norm2", "yT"):
        return 0, 0, 4, 4
    if name in ("z", "bT", "kdT", "swap"):
        return 0, 0, 1, 0
    if name in ("aT", "u", "oC"):
        return 0, 0, 2, 0
    if name == "oCT" or name[0] == "V":
        return 0, 0, 2, 2
    if name[0] in "SP":
        return 0, 0, 4, 0
    if name == "branch":
        return 1, TT, 0, 0
    if name in ("wo", "gate", "up"):
        return 2, TT, 0, 0
    if name == "hT":
        return 0, 0, len(block_pairs(i)), len(block_pairs(i))
    assert name == "down"
    return 2, 2 * TT if i == 0 else 0, 0, 0


FIRST = {}
_at = [0, 0, 0, 0]
for _l in range(LAYERS):
    for _s in STEPS[_l]:
        FIRST[_l, _s] = tuple(_at)
        _at = [a + b for a, b in zip(_at, sizes(_s))]
UNITS0, PROJ0, AUX0, HI0 = _at
ROUTER_AUX = AUX0
GATHER_AUX = AUX0 + 2
AUX0 += 6

RING, LEAD = 5, 3
E_RING, E_LEAD = 8, 4
CAP = 4 * SW
BANKS = 4

E_UNITS = 2 * 2 * NFE + 2 * len(down_groups(FET))
E_PROJ = 2 * NFE + 2
E_AUX = 4 + 4 + 4
E_HI = 4 + 2
MAXPASS = 12
assert 2 * E_UNITS % E_RING == 0 and 2 * E_PROJ % BANKS == 0 and 2 * E_AUX % BANKS == 0


def turned(j):
    return {12: (0, 1), 16: (2,), 18: (3,)}.get(j, ())


LAST_UNIT = {}
for _l in range(LAYERS):
    for _s in STEPS[_l]:
        _u, _b, _, _ = sizes(_s)
        _end = FIRST[_l, _s][0] + _u - 1
        if _s == ("down", 0):
            _end = FIRST[_l, ("down", len(down_groups(FT)) - 1)][0] + 1
        for _n in range(_b):
            LAST_UNIT[FIRST[_l, _s][1] + _n] = _end
for _e in range(2):
    _n, _u = PROJ0 + _e * E_PROJ, UNITS0 + _e * E_UNITS
    for _b in range(2 * NFE):
        LAST_UNIT[_n + _b] = _u + 2 * _b + 1
    for _h in range(2):
        LAST_UNIT[_n + 2 * NFE + _h] = _u + E_UNITS - 2 + _h


def uses(n, size, i=0, per=0):
    return n // size + i * (per // size)


def build(nc, t):
    with ExitStack() as ctx:
        scope = [ctx]

        def sb(name, shape, dt=F32):
            return scope[0].enter_context(nc.sbuf_tensor(name, [P] + shape, dt))

        def sem(name):
            return ctx.enter_context(nc.semaphore(name))

        x = sb("x", [TT, D])
        xhat = sb("xhat", [TT, D])
        hT_hi, hT_lo = sb("hT_hi", [KD, T], F32R), sb("hT_lo", [KD, T], F32R)
        def in_one_place(name_a, name_b, shape):
            outer, scope[0] = scope[0], ExitStack()
            a = sb(name_a, shape)
            scope[0].close()
            scope[0] = outer
            return a, sb(name_b, shape, F32R)

        raw, w_lo = in_one_place("raw", "w_lo", [RING, CAP])
        w_hi = sb("w_hi", [RING, CAP], F32R)
        ident, swap_m = sb("ident", [P]), sb("swap_m", [P])
        mask = sb("mask", [2, 3 * P])
        tri16, tri1, ones = sb("tri16", [P]), sb("tri1", [P]), sb("ones", [P])
        iota = sb("iota", [P])
        wg = sb("wg", [LAYERS, GH * GDK])
        normg = sb("normg", [BW])
        gain = sb("gain", [4 * KD])
        sinks = sb("sinks", [LAYERS * SWA_H])
        router, r_hi, r_lo = sb("router", [KD, NE]), sb("r_hi", [KD, NE], F32R), sb("r_lo", [KD, NE], F32R)
        nrm = sb("nrm", [8, TT])
        gn = sb("gn", [8, 2 * GH])
        qm, ql, qs = sb("qm", [4, 2]), sb("ql", [4, 2]), sb("qs", [4, 2])

        start = ExitStack()
        scope[0] = start
        iota_i, gain_rows = sb("iota_i", [P], I32), sb("gain_rows", [P])
        start.close()

        mix = ExitStack()
        scope[0] = mix
        buf = {
            "aq": sb("aq", [4, T]), "ak": sb("ak", [2, T]), "av": sb("av", [TT, P]),
            "bq": sb("bq", [4, T]), "bk": sb("bk", [4, T]), "bv": sb("bv", [TT, BW]),
            "cq": sb("cq", [2, T]), "ck": sb("ck", [2, T]), "cv": sb("cv", [TT, BW]),
            "cr": sb("cr", [TT, BW]), "cg": sb("cg", [1, T]),
        }
        gl_g, gl_b, gl_n, gl_d = sb("gl_g", [TT, T]), sb("gl_b", [2, T]), sb("gl_n", [2, T]), sb("gl_d", [2, T])
        oc = sb("oc", [TT, BW])
        early = ExitStack()
        scope[0] = early
        aT = sb("aT", [2, 4, P])
        state = sb("state", [3, 2, GDV])
        early.close()
        scope[0] = mix
        pT = sb("pT", [4, 3 * P])
        sb("pT_end", [2 * P])
        oT_hi, oT_lo = sb("oT_hi", [3, 4, T], F32R), sb("oT_lo", [3, 4, T], F32R)
        buf["gates"] = sb("gates", [TT, 3 * D])
        mix.close()

        ffn = ExitStack()
        scope[0] = ffn
        hid = sb("hid", [TT, F])
        hidT_hi, hidT_lo = sb("hidT_hi", [FT, T], F32R), sb("hidT_lo", [FT, T], F32R)
        sg = sb("sg", [TT, FC])
        ffn.close()

        moe = ctx
        scope[0] = moe
        raw_e, w_lo_e = in_one_place("raw_e", "w_lo_e", [E_RING - RING, CAP])
        w_hi_e = sb("w_hi_e", [E_RING - RING, CAP], F32R)
        h_hi, h_lo = sb("h_hi", [TT, D], F32R), sb("h_lo", [TT, D], F32R)
        g_row = sb("g_row", [D])
        sel = sb("sel", [2, TT, P], F32R)
        selT = sb("selT", [T], F32R)
        xe_hi, xe_lo = sb("xe_hi", [2, KD, P], F32R), sb("xe_lo", [2, KD, P], F32R)
        ehid = sb("ehid", [FE])
        ehT_hi, ehT_lo = sb("ehT_hi", [FET, P], F32R), sb("ehT_lo", [FET, P], F32R)
        esg = sb("esg", [2, FC])
        y_hi, y_lo = sb("y_hi", [D], F32R), sb("y_lo", [D], F32R)
        pslot = sb("pslot", [1])
        lg, oh1, oh2, rt = sb("lg", [TT, NE]), sb("oh1", [TT, NE]), sb("oh2", [TT, NE]), sb("rt", [TT, NE])
        comb, slots = sb("comb", [TT, MAXPASS + 2]), sb("slots", [TT, MAXPASS + 2])
        picked = sb("picked", [TT, NE])
        ti = sb("ti", [8, TT])
        cnt, over, rank, oj, ot = (sb(n, [NE]) for n in ("cnt", "over", "rank", "oj", "ot"))
        ids_f, ids = sb("ids_f", [8]), sb("ids", [8], I32)

        ps = ctx.enter_context(nc.psum_tensor("ps", [P, 2 * BANKS, 512], F32))

        s_x, s_gain, s_small = sem("s_x"), sem("s_gain"), sem("s_small")
        s_normg = sem("s_normg")
        normg_used = sem("normg_used")
        s_grow = sem("s_grow")
        loaded = [sem(f"loaded{i}") for i in range(RING)]
        loaded_e = [sem(f"loaded_e{i}") for i in range(E_RING)]
        hi_done, lo_done, w_used = sem("hi_done"), sem("lo_done"), sem("w_used")
        consts = sem("consts")
        pool_seq = sem("pool_seq")
        aux_done = sem("aux_done")
        proj_free = [sem(f"proj_free{i}") for i in range(BANKS)]
        aux_free = [sem(f"aux_free{i}") for i in range(BANKS)]
        part_hi = sem("part_hi")
        dseq, aseq = sem("dseq"), sem("aseq")
        sq_sum, mean_sq, root = sem("sq_sum"), sem("mean_sq"), sem("root")
        xhat_done = sem("xhat_done")
        gain_ready, gain_done = sem("gain_ready"), sem("gain_done")
        z_ln, b_ready, b_exp, gla_qk = sem("z_ln"), sem("b_ready"), sem("b_exp"), sem("gla_qk")
        gn_sum, gn_mean, gn_root, oc_ready = sem("gn_sum"), sem("gn_mean"), sem("gn_root"), sem("oc_ready")
        state_ready = sem("state_ready")
        q_max, q_exp, q_prob = sem("q_max"), sem("q_exp"), sem("q_prob")
        cg_ones, y_ready = sem("cg_ones"), sem("y_ready")
        router_split, picked_ready, diff_ready, e_ready = (
            sem("router_split"), sem("picked_ready"), sem("diff_ready"), sem("e_ready"))
        h_ready, h_hi_ready = sem("h_ready"), sem("h_hi_ready")
        route_ready = sem("route_ready")
        sel_ready, pslot_ready, moe_zero, x_sum = sem("sel_ready"), sem("pslot_ready"), sem("moe_zero"), sem("x_sum")
        out_ready, s_out = sem("out_ready"), sem("s_out")

        block = ctx.enter_context(nc.Block())

        def slot(n, part, size):
            at = (n - UNITS0) % E_RING
            if n >= UNITS0 and at < E_RING - RING:
                return {"raw": raw_e, "hi": w_hi_e, "lo": w_lo_e}[part][:, at, 0:size]
            at = n % RING if n < UNITS0 else (UNITS0 + at - E_RING) % RING
            return {"raw": raw, "hi": w_hi, "lo": w_lo}[part][:, at, 0:size]

        def unit(n, part, k, w):
            return slot(n, part, k * w).rearrange("p (k c) -> p k c", k=k)

        def load_of(n, i=0):
            if n < UNITS0:
                return loaded[n % RING], 16 * (n // RING + 1)
            m = n - UNITS0
            return loaded_e[m % E_RING], 16 * (m // E_RING + 1 + i * (2 * E_UNITS // E_RING))

        def proj_bank(n):
            return ps[:, n % BANKS, :]

        def aux_bank(n):
            return ps[:, BANKS + n % BANKS, :]

        def projected(eng, n, i=0):
            eng.wait_ge(w_used, LAST_UNIT[n] + 1 + i * 2 * E_UNITS)

        def aux_filled(eng, n, i=0, per=0):
            eng.wait_ge(aux_done, n + 1 + i * per)

        def proj_read(eng, n, i=0, per=0):
            eng.wait_ge(proj_free[n % BANKS], uses(n, BANKS, i, per) + 1)

        def aux_read(eng, n, i=0, per=0):
            eng.wait_ge(aux_free[n % BANKS], uses(n, BANKS, i, per) + 1)

        def slab_read(eng, l, name):
            first = FIRST[l, (name, 0)][1]
            for b in range(len(SLABS[name][2])):
                proj_read(eng, first + b)

        def k_cut(w, k0, k, c0, c):
            return w[k0 * P:(k0 + k) * P, c0:c0 + c].rearrange("(k p) c -> p k c", p=P)

        static_units = []
        for l in range(LAYERS):
            for name, i in STEPS[l]:
                if name in SLABS:
                    c0, w, _ = SLABS[name]
                    static_units += [(k_cut(t["w_in"][l], 4 * kh, 4, c0, w), 4, w) for kh in range(2)]
                elif name == "branch":
                    c0, w = WCOLS[i % 3]
                    static_units.append((k_cut(t["w_branch_" + "abc"[i // 3]][l], 0, 4, c0, w), 4, w))
                elif name == "wo":
                    c0, w = WCOLS[i]
                    static_units += [(k_cut(t["w_o"][l], 4 * kh, 4, c0, w), 4, w) for kh in range(2)]
                elif name in ("gate", "up"):
                    static_units += [(k_cut(t["ffn_w_" + name][l // 2], 4 * kh, 4, FC * i, FC), 4, FC)
                                     for kh in range(2)]
                elif name == "down":
                    k0, k = down_groups(FT)[i]
                    static_units += [(k_cut(t["ffn_w_down"][l // 2], k0, k, HALF * h, HALF), k, HALF)
                                     for h in range(2)]
        assert len(static_units) == UNITS0

        e_units = []
        for c in range(NFE):
            for which in ("gate", "up"):
                e_units += [(which, 4 * kh, 4, FC * c, FC) for kh in range(2)]
        for k0, k in down_groups(FET):
            e_units += [("down", k0, k, HALF * h, HALF) for h in range(2)]
        assert len(e_units) == E_UNITS

        def unit_size(n):
            if n < UNITS0:
                return static_units[n][1] * static_units[n][2]
            _, _, k, _, c = e_units[(n - UNITS0) % E_UNITS]
            return k * c

        @block.sync
        def _(sp):
            for tt in range(TT):
                sp.dma_start(x[:, tt, :], t["x"][0, tt * P:(tt + 1) * P, :]).then_inc(s_x, 16)
            sp.dma_start(gain_rows[0:16, :], t["norm1_g"].rearrange("l (k p) -> (l k) p", p=P)).then_inc(s_gain, 16)
            sp.dma_start(gain_rows[16:32, :], t["norm2_g"].rearrange("l (k p) -> (l k) p", p=P)).then_inc(s_gain, 16)

            def load(n, src, k, w, i=0):
                before = n - (RING if n < UNITS0 else E_RING)
                if before >= 0:
                    sp.wait_ge(w_used, before + 1 + i * 2 * E_UNITS)
                sp.dma_start(unit(n, "raw", k, w), src).then_inc(load_of(n)[0], 16)

            def expert_unit(j, e):
                which, k0, k, c0, c = e_units[j]
                return k_cut(t["moe_w_" + which][0, e], k0, k, c0, c), k, c

            for n, (src, k, w) in enumerate(static_units):
                load(n, src, k, w)
                if n == 1:
                    sp.dma_start(wg[0:GRANK, :, :], t["gla_w_gate"].rearrange("l r c -> r l c")).then_inc(s_small, 16)
                    sp.dma_start(wg[GRANK:GRANK + 1, :, :], t["gla_b_gate"].unsqueeze(0)).then_inc(s_small, 16)
                    sp.dma_start(sinks[:, :], t["swa_sinks"].rearrange("l h -> (l h)").partition_broadcast(P)).then_inc(s_small, 16)
                    sp.dma_start(router[:, :, :], t["moe_router"][0].rearrange("(k p) e -> p k e", p=P)).then_inc(s_small, 16)
                    sp.dma_start(normg[:, :], t["gla_norm_g"][0].partition_broadcast(P)).then_inc(s_normg, 16)
                if n == FIRST[1, ("C4", 0)][0] + 1:
                    sp.wait_ge(normg_used, 1)
                    sp.dma_start(normg[:, :], t["gla_norm_g"][1].partition_broadcast(P)).then_inc(s_normg, 16)
            sp.wait_ge(aux_done, FIRST[1, ("V3", 0)][2] + 2)
            with sp.Fori(0, NE // 2) as i:
                for s in range(2):
                    for j in range(E_UNITS):
                        load(UNITS0 + s * E_UNITS + j, *expert_unit(j, i * 2 + s), i=i)
            sp.wait_ge(route_ready, 1)
            iters = sp.value_load(ids[0:1, 7:8], min_val=NE // 2, max_val=MAXPASS // 2)
            with sp.If(iters > NE // 2):
                with sp.Fori(NE // 2, iters) as i:
                    first = sp.value_load(ids[0:1, bass.ds((i - NE // 2) * 2, 1)], min_val=0, max_val=NE - 1)
                    second = sp.value_load(ids[0:1, bass.ds((i - NE // 2) * 2 + 1, 1)], min_val=0, max_val=NE - 1)
                    for s, e in enumerate((first, second)):
                        for j in range(E_UNITS):
                            load(UNITS0 + s * E_UNITS + j, *expert_unit(j, e), i=i)
            for j in range(E_LEAD):
                load(UNITS0 + j, *expert_unit(j, 0), i=iters)
            sp.wait_ge(out_ready, TT)
            for tt in range(TT):
                sp.dma_start(t["out"][0, tt * P:(tt + 1) * P, :], xhat[:, tt, :]).then_inc(s_out, 16)
            sp.wait_ge(s_out, 16 * TT)

        @block.gpsimd
        def _(pool):
            seq = [0]

            def link(ins):
                seq[0] += 1
                ins.then_inc(pool_seq, 1)
                pool.wait_ge(pool_seq, seq[0])

            def select(out, op, base, pattern, fill, mult):
                return pool.affine_select(out=out, in_=out, compare_op=op, fill=fill, base=base,
                                          pattern=pattern, channel_multiplier=mult)

            pool.memset(ident[:, :], 0.0)
            pool.memset(swap_m[:, :], 0.0)
            pool.memset(mask[:, :, :], 0.0)
            pool.memset(tri16[:, :], 1.0 / 16.0)
            pool.memset(tri1[:, :], 1.0)
            pool.memset(ones[:, :], 1.0)
            link(pool.iota(iota_i[:, :], pattern=[[1, P]], base=0, channel_multiplier=0))
            link(select(ident[:, :], ALU.not_equal, 0, [[-1, P]], 1.0, 1))
            link(select(swap_m[:, 0:64], ALU.not_equal, -64, [[-1, 64]], 1.0, 1))
            link(select(swap_m[:, 64:128], ALU.not_equal, 0, [[-1, 64]], 1.0, 1))
            for b in range(2):
                for blk in (0, 2):
                    link(select(mask[:, b, blk * P:(blk + 1) * P], ALU.is_ge, 0, [[-1, P]], NEG, 1))
            link(select(mask[:, 0, P:2 * P], ALU.is_gt, 0, [[1, P]], NEG, -1))
            link(select(tri1[:, :], ALU.is_ge, 0, [[1, P]], 0.0, -1))
            link(select(tri16[:, :], ALU.is_ge, 0, [[1, P]], 0.0, -1))
            link(pool.memset(tri16[0:64, 64:128], 0.0))
            pool.tensor_copy(iota[:, :], iota_i[:, :]).then_inc(consts, 1)

        @block.scalar
        def _(act):
            seq = [0]

            def link(ins):
                seq[0] += 1
                ins.then_inc(aseq, 1)
                act.wait_ge(aseq, seq[0])

            def split_hi(n, i=0):
                k = unit_size(n)
                act.wait_ge(*load_of(n, i))
                act.activation(slot(n, "hi", k), slot(n, "raw", k), ACT.Copy).then_inc(hi_done, 1)

            def squares(tt, m):
                act.activation(xhat[:, tt, :], x[:, tt, :], ACT.Square,
                               accum_out=nrm[:, 0, tt:tt + 1]).then_inc(sq_sum, 1)

            def norm(m, ready):
                for tt in range(TT):
                    ready(tt)
                    squares(tt, m)
                act.wait_ge(mean_sq, m + 1)
                act.activation(nrm[:, 2, :], nrm[:, 1, :], ACT.Sqrt).then_inc(root, 1)

            def gained_hi(l, step, m):
                _, _, a, _ = FIRST[l, step]
                for g in range(4):
                    aux_filled(act, a + g)
                    for kk in range(2):
                        k = 2 * g + kk
                        ins = act.activation(hT_hi[:, k, :], aux_bank(a + g)[:, kk * T:(kk + 1) * T],
                                             ACT.Copy, scale=gain[:, m * KD + k:m * KD + k + 1])
                    ins.then_inc(part_hi, 1)

            for n in range(LEAD):
                split_hi(n)
            for l in range(LAYERS):
                for step in STEPS[l]:
                    name, i = step
                    n, p, a, _ = FIRST[l, step]
                    units = sizes(step)[0]
                    for u in range(units):
                        split_hi(n + u + LEAD)
                    if name == "norm":
                        def ready(tt):
                            if l == 0:
                                act.wait_ge(s_x, 16 * TT)
                            else:
                                d = FIRST[0, ("down", 0)][1]
                                for h in range(2):
                                    proj_read(act, d + 2 * tt + h)
                        norm(2 * l, ready)
                        if l == 0:
                            act.wait_ge(gain_ready, 1)
                            act.activation(gain[:, :], aux_bank(BANKS - 1)[:, 0:4 * KD], ACT.Copy).then_inc(gain_done, 1)
                            act.wait_ge(gain_done, 1)
                        gained_hi(l, step, l)
                    elif name == "norm2":
                        def ready(tt):
                            for s in range(3):
                                proj_read(act, FIRST[l, ("wo", s)][1] + tt)
                        norm(2 * l + 1, ready)
                        gained_hi(l, step, 2 + l)
                    elif name in SLABS:
                        for b, bank in enumerate(SLABS[name][2]):
                            if bank[0] != "t":
                                continue
                            projected(act, p + b)
                            tt = bank[1]
                            for c, w, dst, at in PIECES[name]:
                                func = ACT.Silu if dst == "cr" else ACT.Sigmoid if name in ("G4", "G5", "G6", "G7") else ACT.Copy
                                ins = act.activation(buf[dst][:, tt, at:at + w], proj_bank(p + b)[:, c:c + w], func)
                            ins.then_inc(proj_free[(p + b) % BANKS], 1)
                        if name == "G3":
                            slab_read(act, l, "G3")
                            for tt in range(TT):
                                g = buf["gates"][:, tt, 0:GATE0 + 3 * SW]
                                act.activation(g, g, ACT.Sigmoid)
                    elif name == "z":
                        aux_filled(act, a)
                        zb = gl_b[:, :, :].rearrange("p a b -> p (a b)")
                        link(act.activation(zb, aux_bank(a), ACT.Abs))
                        link(act.activation(zb, zb, ACT.Exp, scale=-1.0))
                        act.activation(zb, zb, ACT.Ln, bias=1.0).then_inc(z_ln, 1)
                    elif name == "bT":
                        act.wait_ge(b_ready, l + 1)
                        act.activation(gl_n[:, :, :], gl_b[:, :, :], ACT.Exp, scale=-1.0)
                        act.activation(gl_d[:, :, :], gl_d[:, :, :], ACT.Exp)
                        act.activation(gl_b[:, :, :], gl_b[:, :, :], ACT.Exp).then_inc(b_exp, 1)
                    elif name == "oC":
                        for par in range(2):
                            aux_filled(act, a + par)
                            for j in range(4):
                                ins = act.activation(oc[:, par, j * GDV:(j + 1) * GDV], aux_bank(a + par)[:, j * GDV:(j + 1) * GDV],
                                                     ACT.Square, accum_out=gn[:, 0, 4 * par + j:4 * par + j + 1])
                        ins.then_inc(gn_sum, 1)
                        act.wait_ge(gn_mean, l + 1)
                        act.activation(gn[:, 2, :], gn[:, 1, :], ACT.Sqrt).then_inc(gn_root, 1)
                    elif name[0] == "S":
                        q = 4 * l + int(name[1])
                        act.wait_ge(q_max, q + 1)
                        sm = xhat[:, :, :].rearrange("p a b -> p (a b)")
                        for h in range(4):
                            for tt in range(TT):
                                at, w = 3 * P * h + P * tt, P * (tt + 1)
                                ins = act.activation(sm[:, at:at + w], sm[:, at:at + w], ACT.Exp,
                                                     bias=qm[:, h, tt:tt + 1], accum_out=ql[:, h, tt:tt + 1])
                        if int(name[1]) < 2:
                            ins = act.activation(qs[:, :, :], qs[:, :, :], ACT.Exp)
                        ins.then_inc(q_exp, 1)
                    elif name[0] == "P":
                        for h in range(4):
                            aux_filled(act, a + h)
                            act.activation(pT[:, h, :], aux_bank(a + h)[:, 0:3 * P], ACT.Copy).then_inc(aux_free[(a + h) % BANKS], 1)
                    elif name[0] == "V" or name == "oCT":
                        br = 2 if name == "oCT" else int(name[1]) // 2
                        for g in range(2):
                            aux_filled(act, a + g)
                            if name == "oCT":
                                out, src = oT_hi[:, 2, 2 * g:2 * g + 2, :], aux_bank(a + g).rearrange("p (a b) -> p a b", a=2)
                            else:
                                out, src = oT_hi[:, br, 2 * (int(name[1]) % 2) + g, :], aux_bank(a + g)[:, 0:T]
                            act.activation(out, src, ACT.Copy).then_inc(part_hi, 1)
                    elif name == "yT":
                        for g in range(4):
                            aux_filled(act, a + g)
                            act.activation(hT_hi[:, 2 * g:2 * g + 2, :], aux_bank(a + g).rearrange("p (a b) -> p a b", a=2),
                                           ACT.Copy).then_inc(part_hi, 1)
                    elif name == "gate":
                        for tt in range(TT):
                            projected(act, p + tt)
                            if i:
                                proj_read(act, FIRST[l, ("up", i - 1)][1] + tt)
                            act.activation(sg[:, tt, :], proj_bank(p + tt)[:, 0:FC], ACT.Silu).then_inc(proj_free[(p + tt) % BANKS], 1)
                    elif name == "hT":
                        for g, (j, m) in enumerate(block_pairs(i)):
                            aux_filled(act, a + g)
                            act.activation(hidT_hi[:, j:j + m, :], aux_bank(a + g)[:, 0:m * T].rearrange("p (a b) -> p a b", a=m),
                                           ACT.Copy).then_inc(part_hi, 1)

            for n in range(LEAD, E_LEAD):
                split_hi(UNITS0 + n)
            act.wait_ge(xhat_done, 8)
            act.dma_start(g_row[:, :], t["norm2_g"][1].partition_broadcast(P)).then_inc(s_grow, 16)
            act.wait_ge(s_small, 64)
            act.activation(r_hi[:, :, :], router[:, :, :], ACT.Copy).then_inc(router_split, 1)
            act.wait_ge(h_ready, 1)
            act.activation(h_hi[:, :, :], xhat[:, :, :], ACT.Copy).then_inc(h_hi_ready, 1)
            act.wait_ge(diff_ready, 1)
            act.activation(ti[:, 5, :], ti[:, 4, :], ACT.Exp).then_inc(e_ready, 1)

            def gather_out(a, dst, i=0):
                for part, out in enumerate((xe_hi, xe_lo)):
                    for g in range(2):
                        n = a + 2 * part + g
                        aux_filled(act, n, i, 2 * E_AUX)
                        act.activation(out[:, dst, 4 * g:4 * g + 4, :], aux_bank(n).rearrange("p (a b) -> p a b", a=4),
                                       ACT.Copy).then_inc(aux_free[n % BANKS], 1)

            act.dma_start(g_row[:, :], t["final_norm_g"].partition_broadcast(P)).then_inc(s_grow, 16)
            gather_out(GATHER_AUX, 0)
            act.wait_ge(route_ready, 1)
            iters = act.value_load(ids[0:1, 7:8], min_val=NE // 2, max_val=MAXPASS // 2)
            with act.Fori(0, iters) as i:
                for s in range(2):
                    n0, p0 = UNITS0 + s * E_UNITS, PROJ0 + s * E_PROJ
                    a0, hi0 = AUX0 + s * E_AUX, HI0 + s * E_HI
                    for j in range(E_UNITS):
                        split_hi(n0 + j + E_LEAD, i)
                        c = j // 4
                        if j < 4 * NFE and j % 4 == 1:
                            n = p0 + 2 * c
                            projected(act, n, i)
                            proj_read(act, n - 3 if c >= 2 else n + 5 - E_PROJ, i, 2 * E_PROJ)
                            act.activation(esg[:, c % 2, :], proj_bank(n)[:, 0:FC], ACT.Silu).then_inc(proj_free[n % BANKS], 1)
                        for tr in turned(j):
                            a = a0 + 8 + tr
                            b0, b1 = (blocks_done(tr - 1) if tr else 0), blocks_done(tr)
                            aux_filled(act, a, i, 2 * E_AUX)
                            act.activation(ehT_hi[:, b0:b1, :], aux_bank(a)[:, 0:(b1 - b0) * P].rearrange("p (a b) -> p a b", b=P),
                                           ACT.Copy).then_inc(part_hi, 1)
                        if j == 8:
                            gather_out(a0 + 4, (s + 1) % 2, i)
                    for h in range(2):
                        projected(act, p0 + 2 * NFE + h, i)
                        act.wait_ge(pslot_ready, s + 1 + i * 2)
                        act.activation(y_hi[:, h * HALF:(h + 1) * HALF], proj_bank(p0 + 2 * NFE + h), ACT.Copy,
                                       scale=pslot[:, 0:1]).then_inc(part_hi, 1)

            act.wait_ge(x_sum, 4)
            for tt in range(TT):
                squares(tt, 4)
            act.wait_ge(mean_sq, 5)
            act.activation(nrm[:, 2, :], nrm[:, 1, :], ACT.Sqrt).then_inc(root, 1)

        @block.vector
        def _(dve):
            seq = [0]

            def link(ins):
                seq[0] += 1
                ins.then_inc(dseq, 1)
                dve.wait_ge(dseq, seq[0])

            def split_lo(n, i=0):
                k = unit_size(n)
                dve.wait_ge(hi_done, n + 1 + i * 2 * E_UNITS)
                dve.tensor_tensor(slot(n, "lo", k), slot(n, "raw", k), slot(n, "hi", k).bitcast(F32),
                                  ALU.subtract).then_inc(lo_done, 1)

            def part_lo(out, src, hi, number, i=0, scale=1.0):
                dve.wait_ge(part_hi, number + 1 + (i * 2 * E_HI))
                return dve.scalar_tensor_tensor(out=out, in0=src, scalar=scale, in1=hi.bitcast(F32),
                                                op0=ALU.mult, op1=ALU.subtract)

            def rsqrt(v, m, sums, means, roots, width):
                dve.wait_ge(sums[0], sums[1])
                dve.tensor_scalar(v[:, 1, :], v[:, 0, :], 1.0 / width, EPS, ALU.mult, ALU.add).then_inc(means, 1)
                dve.wait_ge(means, m + 1)
                dve.wait_ge(roots, m + 1)
                link(dve.reciprocal(v[:, 3, :], v[:, 2, :]))
                link(dve.tensor_tensor(v[:, 4, :], v[:, 1, :], v[:, 3, :], ALU.mult))
                link(dve.tensor_tensor(v[:, 4, :], v[:, 4, :], v[:, 3, :], ALU.mult))
                link(dve.tensor_scalar(v[:, 4, :], v[:, 4, :], -0.5, 1.5, ALU.mult, ALU.add))
                link(dve.tensor_tensor(v[:, 3, :], v[:, 4, :], v[:, 3, :], ALU.mult))

            def norm(m):
                rsqrt(nrm, m, (sq_sum, 2 * m + 2), mean_sq, root, D)
                for tt in range(TT):
                    dve.tensor_scalar(xhat[:, tt, :], x[:, tt, :], nrm[:, 3, tt:tt + 1], None, ALU.mult).then_inc(xhat_done, 1)

            def gained_lo(a, hi0, m):
                if m == 0:
                    dve.wait_ge(gain_done, 1)
                for g in range(4):
                    for kk in range(2):
                        k = 2 * g + kk
                        ins = part_lo(hT_lo[:, k, :], aux_bank(a + g)[:, kk * T:(kk + 1) * T], hT_hi[:, k, :], hi0 + g,
                                      scale=gain[:, m * KD + k:m * KD + k + 1])
                    ins.then_inc(aux_free[(a + g) % BANKS], 1)

            dve.memset(buf["cg"][:, :, :], 1.0).then_inc(cg_ones, 1)
            for n in range(LEAD):
                split_lo(n)
            dve.wait_ge(consts, 1)
            dve.wait_ge(cg_ones, 1)
            for l in range(LAYERS):
                for step in STEPS[l]:
                    name, i = step
                    n, p, a, hi0 = FIRST[l, step]
                    for u in range(sizes(step)[0]):
                        split_lo(n + u + LEAD)
                    if name == "norm":
                        norm(2 * l)
                        gained_lo(a, hi0, l)
                        if l == 1:
                            link(dve.memset(buf["cg"][:, :, :], 1.0))
                        link(dve.memset(aT[:, :, :, :], 0.0))
                    elif name == "norm2":
                        norm(2 * l + 1)
                        gained_lo(a, hi0, 2 + l)
                    elif name in SLABS:
                        for b, bank in enumerate(SLABS[name][2]):
                            if bank[0] == "t":
                                continue
                            _, _, blocks, dst, at = bank
                            projected(dve, p + b)
                            rows = GRANK if bank[0] == "g" else P
                            dve.tensor_copy(buf[dst][0:rows, at:at + blocks, :],
                                            proj_bank(p + b)[0:rows, 0:blocks * T].rearrange("p (a b) -> p a b", a=blocks)
                                            ).then_inc(proj_free[(p + b) % BANKS], 1)
                        if name == "C3":
                            slab_read(dve, l, "C2")
                            slab_read(dve, l, "C3")
                            dve.wait_ge(s_normg, 16 * (l + 1))
                            dve.tensor_tensor(buf["cr"][:, :, :], buf["cr"][:, :, :],
                                              normg[:, :].unsqueeze(1).broadcast_to([P, TT, BW]), ALU.mult).then_inc(normg_used, 1)
                    elif name == "z":
                        dve.wait_ge(z_ln, l + 1)
                        dve.scalar_tensor_tensor(out=gl_g[:, :, :].rearrange("p a b -> p (a b)"), in0=aux_bank(a), scalar=0.0,
                                                 in1=gl_b[:, :, :].rearrange("p a b -> p (a b)"),
                                                 op0=ALU.min, op1=ALU.subtract).then_inc(aux_free[a % BANKS], 1)
                    elif name == "bT":
                        aux_filled(dve, a)
                        bb = gl_b[:, :, :].rearrange("p a b -> p (a b)")
                        dve.tensor_copy(bb, aux_bank(a)).then_inc(aux_free[a % BANKS], 1)
                        aux_read(dve, a)
                        chunks = bb.rearrange("p (n c) -> p n c", c=CH)
                        dve.tensor_tensor(gl_d[:, :, :].rearrange("p a b -> p (a b)").rearrange("p (n c) -> p n c", c=CH),
                                          chunks[:, :, CH - 1:CH].broadcast_to([P, 2 * T // CH, CH]), chunks,
                                          ALU.subtract).then_inc(b_ready, 1)
                        slab_read(dve, l, "C0")
                        slab_read(dve, l, "C1")
                        dve.wait_ge(b_exp, l + 1)
                        cq, ck = buf["cq"], buf["ck"]
                        fl = lambda v: v[:, :, :].rearrange("p a b -> p (a b)")
                        dve.scalar_tensor_tensor(out=fl(cq), in0=fl(cq), scalar=GDK ** -0.5, in1=fl(gl_b), op0=ALU.mult, op1=ALU.mult)
                        dve.tensor_tensor(fl(gl_n), fl(ck), fl(gl_n), ALU.mult)
                        dve.tensor_tensor(fl(gl_d), fl(ck), fl(gl_d), ALU.mult).then_inc(gla_qk, 1)
                    elif name == "kdT":
                        aux_filled(dve, a)
                        dve.tensor_copy(gl_g[:, :, :].rearrange("p a b -> p (a b)"), aux_bank(a)).then_inc(aux_free[a % BANKS], 1)
                    elif name == "aT":
                        for par in range(2):
                            aux_filled(dve, a + par)
                            dve.copy_predicated(aT[:, par, :, :], tri16[:, :].bitcast(U32).unsqueeze(1).broadcast_to([P, 4, P]),
                                                aux_bank(a + par).rearrange("p (a b) -> p a b", a=4)).then_inc(aux_free[(a + par) % BANKS], 1)
                    elif name == "u":
                        for g in range(2):
                            aux_filled(dve, a + g)
                        u02, u1 = aux_bank(a), aux_bank(a + 1)
                        link(dve.tensor_copy(state[:, 0, :, :].rearrange("p a b -> p (a b)"), u02[:, 0:2 * GDV]))
                        for c in (1, 2):
                            src = u1[:, 0:2 * GDV] if c == 1 else u02[:, 2 * GDV:4 * GDV]
                            for b in range(2):
                                ins = dve.scalar_tensor_tensor(out=state[:, c, b, :], in0=state[:, c - 1, b, :],
                                                               scalar=gl_b[:, b, (c + 1) * CH - 1:(c + 1) * CH],
                                                               in1=src[:, b * GDV:(b + 1) * GDV], op0=ALU.mult, op1=ALU.add)
                                if b == 0:
                                    link(ins)
                            ins.then_inc(aux_free[(a + 2 - c) % BANKS], 1)
                            aux_read(dve, a + 2 - c)
                    elif name == "swap":
                        aux_filled(dve, a)
                        dve.tensor_copy(buf["ak"][:, 1, :], aux_bank(a)[:, 0:T]).then_inc(aux_free[a % BANKS], 1)
                    elif name == "oC":
                        rsqrt(gn, l, (gn_sum, l + 1), gn_mean, gn_root, GDV)
                        for par in range(2):
                            out = oc[:, :, :].rearrange("p t (b q d) -> p (t b) q d", b=2, q=2)[:, :, par, :]
                            dve.tensor_tensor(out, aux_bank(a + par).rearrange("p (j d) -> p j d", j=4),
                                              gn[:, 3, 4 * par:4 * par + 4].unsqueeze(2).broadcast_to([P, 4, GDV]),
                                              ALU.mult).then_inc(aux_free[(a + par) % BANKS], 1)
                            aux_read(dve, a + par)
                        dve.tensor_tensor(oc[:, :, :], oc[:, :, :], buf["cr"][:, :, :], ALU.mult).then_inc(oc_ready, 1)
                    elif name[0] == "S":
                        quad = int(name[1])
                        q = 4 * l + quad
                        sm = xhat[:, :, :].rearrange("p a b -> p (a b)")[:, 0:12 * P].rearrange("p (h c) -> p h c", h=4)
                        for h in range(4):
                            aux_filled(dve, a + h)
                            dve.scalar_tensor_tensor(out=sm[:, h, :], in0=aux_bank(a + h)[:, 0:3 * P], scalar=DH ** -0.5,
                                                     in1=mask[:, quad // 2, :], op0=ALU.mult, op1=ALU.add
                                                     ).then_inc(aux_free[(a + h) % BANKS], 1)
                        aux_read(dve, a + 3)
                        dve.tensor_reduce(qm[:, :, 0:1], sm[:, :, 0:P], AX.X, ALU.max)
                        link(dve.tensor_reduce(qm[:, :, 1:2], sm[:, :, P:3 * P], AX.X, ALU.max))
                        if quad < 2:
                            if q == 0:
                                dve.wait_ge(s_small, 64)
                            s0 = SWA_H * l + 4 * quad
                            sk = sinks[:, s0:s0 + 4].unsqueeze(2).broadcast_to([P, 4, 2])
                            link(dve.tensor_tensor(qm[:, :, :], qm[:, :, :], sk, ALU.max))
                            link(dve.tensor_scalar(qm[:, :, :], qm[:, :, :], -1.0, None, ALU.mult))
                            dve.tensor_tensor(qs[:, :, :], qm[:, :, :], sk, ALU.add).then_inc(q_max, 1)
                        else:
                            dve.tensor_scalar(qm[:, :, :], qm[:, :, :], -1.0, None, ALU.mult).then_inc(q_max, 1)
                        dve.wait_ge(q_exp, q + 1)
                        if quad < 2:
                            link(dve.tensor_tensor(ql[:, :, :], ql[:, :, :], qs[:, :, :], ALU.add))
                        link(dve.reciprocal(ql[:, :, :], ql[:, :, :]))
                        dve.tensor_tensor(sm[:, :, 0:P], sm[:, :, 0:P], ql[:, :, 0:1].broadcast_to([P, 4, P]), ALU.mult)
                        dve.tensor_tensor(sm[:, :, P:3 * P], sm[:, :, P:3 * P], ql[:, :, 1:2].broadcast_to([P, 4, 2 * P]),
                                          ALU.mult).then_inc(q_prob, 1)
                    elif name[0] == "V" or name == "oCT":
                        for g in range(2):
                            if name == "oCT":
                                out, hi = oT_lo[:, 2, 2 * g:2 * g + 2, :], oT_hi[:, 2, 2 * g:2 * g + 2, :]
                                src = aux_bank(a + g).rearrange("p (a b) -> p a b", a=2)
                            else:
                                br, k = int(name[1]) // 2, 2 * (int(name[1]) % 2) + g
                                out, hi, src = oT_lo[:, br, k, :], oT_hi[:, br, k, :], aux_bank(a + g)[:, 0:T]
                            part_lo(out, src, hi, hi0 + g).then_inc(aux_free[(a + g) % BANKS], 1)
                    elif name == "branch":
                        b, s = i // 3, i % 3
                        c0, w = WCOLS[s]
                        if i == 0:
                            slab_read(dve, l, "G7")
                        for tt in range(TT):
                            projected(dve, p + tt)
                            gate = buf["gates"][:, tt, b * D + c0:b * D + c0 + w]
                            out = xhat[:, tt, c0:c0 + w]
                            tmp = pT[:, 2 * tt:2 * tt + 2, :].rearrange("p a b -> p (a b)")[:, 0:w]
                            dve.tensor_tensor(out if b == 0 else tmp, proj_bank(p + tt)[:, 0:w], gate,
                                              ALU.mult).then_inc(proj_free[(p + tt) % BANKS], 1)
                            if b:
                                proj_read(dve, p + tt)
                                dve.tensor_tensor(out, out, tmp, ALU.add).then_inc(y_ready, 1)
                    elif name == "yT":
                        for g in range(4):
                            part_lo(hT_lo[:, 2 * g:2 * g + 2, :], aux_bank(a + g).rearrange("p (a b) -> p a b", a=2),
                                    hT_hi[:, 2 * g:2 * g + 2, :], hi0 + g).then_inc(aux_free[(a + g) % BANKS], 1)
                    elif name == "wo":
                        c0, w = WCOLS[i]
                        for tt in range(TT):
                            projected(dve, p + tt)
                            dve.tensor_tensor(x[:, tt, c0:c0 + w], proj_bank(p + tt)[:, 0:w], x[:, tt, c0:c0 + w],
                                              ALU.add).then_inc(proj_free[(p + tt) % BANKS], 1)
                    elif name == "up":
                        for tt in range(TT):
                            proj_read(dve, FIRST[l, ("gate", i)][1] + tt)
                            projected(dve, p + tt)
                            dve.tensor_tensor(hid[:, tt, FC * i:FC * (i + 1)], proj_bank(p + tt)[:, 0:FC], sg[:, tt, :],
                                              ALU.mult).then_inc(proj_free[(p + tt) % BANKS], 1)
                    elif name == "hT":
                        for g, (j, m) in enumerate(block_pairs(i)):
                            part_lo(hidT_lo[:, j:j + m, :], aux_bank(a + g)[:, 0:m * T].rearrange("p (a b) -> p a b", a=m),
                                    hidT_hi[:, j:j + m, :], hi0 + g).then_inc(aux_free[(a + g) % BANKS], 1)
                    elif name == "down" and i == len(down_groups(FT)) - 1:
                        d = FIRST[l, ("down", 0)][1]
                        for tt in range(TT):
                            for h in range(2):
                                projected(dve, d + 2 * tt + h)
                                dve.tensor_tensor(x[:, tt, h * HALF:(h + 1) * HALF], proj_bank(d + 2 * tt + h),
                                                  x[:, tt, h * HALF:(h + 1) * HALF],
                                                  ALU.add).then_inc(proj_free[(d + 2 * tt + h) % BANKS], 1)

            for n in range(LEAD, E_LEAD):
                split_lo(UNITS0 + n)
            dve.wait_ge(router_split, 1)
            dve.tensor_tensor(r_lo[:, :, :], router[:, :, :], r_hi[:, :, :].bitcast(F32), ALU.subtract).then_inc(router_split, 1)
            dve.memset(y_hi[:, :].bitcast(F32), 0.0)
            dve.memset(y_lo[:, :].bitcast(F32), 0.0)
            dve.memset(selT[:, :].bitcast(F32), 0.0).then_inc(moe_zero, 1)
            dve.wait_ge(s_grow, 16)
            a = ROUTER_AUX
            aux_filled(dve, a)
            dve.tensor_tensor(xhat[:, :, :], xhat[:, :, :], g_row[:, :].unsqueeze(1).broadcast_to([P, TT, D]),
                              ALU.mult).then_inc(h_ready, 1)
            dve.tensor_copy(lg[:, :, :], aux_bank(a)[:, 0:TT * NE].rearrange("p (a b) -> p a b", a=TT)
                            ).then_inc(aux_free[a % BANKS], 1)
            aux_read(dve, a)

            ids8 = iota[:, 0:NE].unsqueeze(1).broadcast_to([P, TT, NE])

            def col(v):
                return v.unsqueeze(2).broadcast_to([P, TT, NE])

            def first_max(logits, top, onehot):
                link(dve.tensor_reduce(ti[:, top, :].unsqueeze(2), logits, AX.X, ALU.max))
                link(dve.tensor_tensor(rt[:, :, :], logits, col(ti[:, top, :]), ALU.is_equal))
                link(dve.tensor_scalar(rt[:, :, :], rt[:, :, :], -float(NE), float(NE), ALU.mult, ALU.add))
                link(dve.tensor_tensor(rt[:, :, :], rt[:, :, :], ids8, ALU.add))
                link(dve.tensor_reduce(ti[:, 2, :].unsqueeze(2), rt[:, :, :], AX.X, ALU.min))
                link(dve.tensor_tensor(onehot, ids8, col(ti[:, 2, :]), ALU.is_equal))

            first_max(lg[:, :, :], 0, oh1[:, :, :])
            link(dve.scalar_tensor_tensor(out=lg[:, :, :], in0=oh1[:, :, :], scalar=-3.0e38, in1=lg[:, :, :],
                                          op0=ALU.mult, op1=ALU.add))
            first_max(lg[:, :, :], 1, oh2[:, :, :])
            dve.tensor_tensor(picked[:, :, :], oh1[:, :, :], oh2[:, :, :], ALU.add).then_inc(picked_ready, 1)
            dve.tensor_tensor(ti[:, 4, :], ti[:, 1, :], ti[:, 0, :], ALU.subtract).then_inc(diff_ready, 1)
            dve.wait_ge(h_hi_ready, 1)
            dve.tensor_tensor(h_lo[:, :, :], xhat[:, :, :], h_hi[:, :, :].bitcast(F32), ALU.subtract).then_inc(h_ready, 1)
            aux_filled(dve, a + 1)
            link(dve.tensor_tensor(rt[:, :, :], aux_bank(a + 1)[:, 0:TT * NE].rearrange("p (a b) -> p a b", a=TT),
                                   picked[:, :, :], ALU.mult))
            dve.tensor_copy(cnt[:, :], aux_bank(a + 1)[:, TT * NE:(TT + 1) * NE]).then_inc(aux_free[(a + 1) % BANKS], 1)
            aux_read(dve, a + 1)
            dve.memset(slots[:, :, :], -1.0)
            link(dve.memset(comb[:, :, :], 0.0))
            link(dve.tensor_scalar(slots[:, :, 0:NE], rt[:, :, :], -1.0, None, ALU.add))
            dve.wait_ge(e_ready, 1)
            link(dve.tensor_scalar(ti[:, 6, :], ti[:, 5, :], 1.0, None, ALU.add))
            link(dve.reciprocal(ti[:, 6, :], ti[:, 6, :]))
            link(dve.tensor_tensor(ti[:, 7, :], ti[:, 5, :], ti[:, 6, :], ALU.mult))
            link(dve.tensor_tensor(oh1[:, :, :], oh1[:, :, :], col(ti[:, 6, :]), ALU.mult))
            link(dve.tensor_tensor(oh2[:, :, :], oh2[:, :, :], col(ti[:, 7, :]), ALU.mult))
            link(dve.tensor_tensor(comb[:, :, 0:NE], oh1[:, :, :], oh2[:, :, :], ALU.add))

            def select(dst, column):
                for tt in range(TT):
                    ins = dve.tensor_scalar(sel[:, dst, tt, :], iota[:, :], slots[:, tt, column], None, ALU.is_equal)
                ins.then_inc(sel_ready, 1)

            select(0, slice(0, 1))
            link(dve.tensor_scalar(over[:, :], cnt[:, :], float(P), None, ALU.is_gt))
            link(dve.tensor_copy(rank[:, 0:1], over[:, 0:1]))
            for e in range(1, NE):
                link(dve.tensor_tensor(rank[:, e:e + 1], rank[:, e - 1:e], over[:, e:e + 1], ALU.add))
            link(dve.tensor_tensor(rank[:, :], rank[:, :], over[:, :], ALU.mult))
            link(dve.memset(ids_f[:, :], 0.0))
            for j in range(MAXPASS - NE):
                link(dve.tensor_scalar(oj[:, :], rank[:, :], float(j + 1), None, ALU.is_equal))
                oje = oj[:, :].unsqueeze(1).broadcast_to([P, TT, NE])
                link(dve.tensor_tensor(ot[:, :], oj[:, :], iota[:, 0:NE], ALU.mult))
                link(dve.tensor_reduce(ids_f[:, j:j + 1], ot[:, :], AX.X, ALU.add))
                link(dve.tensor_tensor(rt[:, :, :], slots[:, :, 0:NE], oje, ALU.mult))
                link(dve.tensor_reduce(slots[:, :, NE + j:NE + j + 1], rt[:, :, :], AX.X, ALU.add))
                link(dve.tensor_scalar(slots[:, :, NE + j:NE + j + 1], slots[:, :, NE + j:NE + j + 1], -float(P), None, ALU.add))
                link(dve.tensor_tensor(rt[:, :, :], comb[:, :, 0:NE], oje, ALU.mult))
                link(dve.tensor_reduce(comb[:, :, NE + j:NE + j + 1], rt[:, :, :], AX.X, ALU.add))
            link(dve.tensor_reduce(ids_f[:, 5:6], rank[:, :], AX.X, ALU.max))
            link(dve.tensor_scalar(ids_f[:, 6:7], ids_f[:, 5:6], 0.0, float(NE // 2), ALU.is_gt, ALU.add))
            link(dve.tensor_scalar(ids_f[:, 7:8], ids_f[:, 5:6], 2.0, None, ALU.is_gt))
            link(dve.tensor_tensor(ids_f[:, 7:8], ids_f[:, 7:8], ids_f[:, 6:7], ALU.add))
            dve.tensor_copy(ids[:, :], ids_f[:, :]).then_inc(route_ready, 1)
            dve.wait_ge(route_ready, 1)
            iters = dve.value_load(ids[0:1, 7:8], min_val=NE // 2, max_val=MAXPASS // 2)

            with dve.Fori(0, iters) as i:
                for s in range(2):
                    n0, p0 = UNITS0 + s * E_UNITS, PROJ0 + s * E_PROJ
                    a0, hi0 = AUX0 + s * E_AUX, HI0 + s * E_HI
                    for j in range(E_UNITS):
                        split_lo(n0 + j + E_LEAD, i)
                        if j == 0:
                            aux_filled(dve, a0 - 3, i, 2 * E_AUX)
                            select((s + 1) % 2, bass.ds(i * 2 + s + 1, 1))
                        c = j // 4
                        if j < 4 * NFE and j % 4 == 3:
                            n = p0 + 2 * c + 1
                            proj_read(dve, n - 1, i, 2 * E_PROJ)
                            projected(dve, n, i)
                            dve.tensor_tensor(ehid[:, FC * c:FC * (c + 1)], proj_bank(n)[:, 0:FC], esg[:, c % 2, :],
                                              ALU.mult).then_inc(proj_free[n % BANKS], 1)
                        if j == 4:
                            for g in range(4):
                                tt, h = g // 2, g % 2
                                aux_filled(dve, a0 + g, i, 2 * E_AUX)
                                xs = x[:, tt, h * HALF:(h + 1) * HALF]
                                dve.tensor_tensor(xs, aux_bank(a0 + g), xs, ALU.add).then_inc(aux_free[(a0 + g) % BANKS], 1)
                        for tr in turned(j):
                            a = a0 + 8 + tr
                            b0, b1 = (blocks_done(tr - 1) if tr else 0), blocks_done(tr)
                            w = (b1 - b0) * P
                            aux_filled(dve, a, i, 2 * E_AUX)
                            dve.wait_ge(part_hi, hi0 + tr + 1 + i * 2 * E_HI)
                            if tr == 0:
                                dve.tensor_copy(selT[:, :], aux_bank(a)[:, w:w + T])
                            if tr == 1:
                                dve.tensor_copy(pslot[:, :], aux_bank(a)[:, w:w + 1]).then_inc(pslot_ready, 1)
                            part_lo(ehT_lo[:, b0:b1, :], aux_bank(a)[:, 0:w].rearrange("p (a b) -> p a b", b=P),
                                    ehT_hi[:, b0:b1, :], hi0 + tr, i).then_inc(aux_free[a % BANKS], 1)
                    for h in range(2):
                        n = p0 + 2 * NFE + h
                        dve.wait_ge(pslot_ready, s + 1 + i * 2)
                        part_lo(y_lo[:, h * HALF:(h + 1) * HALF], proj_bank(n), y_hi[:, h * HALF:(h + 1) * HALF],
                                hi0 + 4 + h, i, scale=pslot[:, 0:1]).then_inc(proj_free[n % BANKS], 1)

            for g in range(4):
                tt, h = g // 2, g % 2
                aux_filled(dve, AUX0 + g, iters, 2 * E_AUX)
                xs = x[:, tt, h * HALF:(h + 1) * HALF]
                dve.tensor_tensor(xs, aux_bank(AUX0 + g), xs, ALU.add).then_inc(x_sum, 1)

            dve.wait_ge(x_sum, 4)
            rsqrt(nrm, 4, (sq_sum, 10), mean_sq, root, D)
            dve.wait_ge(s_grow, 32)
            for tt in range(TT):
                dve.scalar_tensor_tensor(out=xhat[:, tt, :], in0=x[:, tt, :], scalar=nrm[:, 3, tt:tt + 1], in1=g_row[:, :],
                                         op0=ALU.mult, op1=ALU.mult).then_inc(out_ready, 1)

        @block.tensor
        def _(pe):
            def proj_take(n, i=0, per=0):
                if n >= BANKS:
                    pe.wait_ge(proj_free[n % BANKS], uses(n, BANKS, i, per))

            def aux_take(n, i=0, per=0):
                if n >= BANKS:
                    pe.wait_ge(aux_free[n % BANKS], uses(n, BANKS, i, per))

            def unit_ready(n, i=0):
                pe.wait_ge(lo_done, n + 1 + i * 2 * E_UNITS)

            def token_major(out, hi, lo, wh, wl, first, last):
                pe.matmul(out, hi, wh, start=first, stop=False, skip_group_check=True)
                pe.matmul(out, hi, wl, start=False, stop=False, skip_group_check=True)
                return pe.matmul(out, lo, wh, start=False, stop=last, skip_group_check=True)

            def feature_major(out, hi, lo, wh, wl, first, last):
                pe.matmul(out, wh, hi, start=first, stop=False, skip_group_check=True)
                pe.matmul(out, wh, lo, start=False, stop=False, skip_group_check=True)
                return pe.matmul(out, wl, hi, start=False, stop=last, skip_group_check=True)

            def plain(out, lhsT, rhs, start=True, stop=True):
                return pe.matmul(out, lhsT, rhs, start=start, stop=stop, skip_group_check=True)

            def rows_T(a, src):
                for g in range(4):
                    aux_take(a + g)
                    for kk in range(2):
                        k = 2 * g + kk
                        for tt in range(TT):
                            ins = pe.transpose(aux_bank(a + g)[:, kk * T + tt * P:kk * T + (tt + 1) * P],
                                               src[:, tt, k * P:(k + 1) * P], ident[:, :])
                    ins.then_inc(aux_done, 1)

            pe.wait_ge(consts, 1)
            pe.wait_ge(s_gain, 32)
            pe.transpose(aux_bank(BANKS - 1)[:, 0:4 * KD], gain_rows[0:4 * KD, :], ident[0:4 * KD, 0:4 * KD]).then_inc(gain_ready, 1)
            for l in range(LAYERS):
                for step in STEPS[l]:
                    name, i = step
                    n, p, a, _ = FIRST[l, step]
                    if name in ("norm", "norm2"):
                        pe.wait_ge(xhat_done, 2 * (2 * l + (name == "norm2")) + 2)
                        if l == 0 and name == "norm":
                            pe.wait_ge(gain_done, 1)
                        rows_T(a, xhat)
                        for g in range(4):
                            aux_read(pe, a + g)
                    elif name in SLABS:
                        _, w, banks = SLABS[name]
                        for b in range(len(banks)):
                            proj_take(p + b)
                        for kh in range(2):
                            unit_ready(n + kh)
                            wh, wl = unit(n + kh, "hi", 4, w), unit(n + kh, "lo", 4, w)
                            for kk in range(4):
                                k = 4 * kh + kk
                                for b, bank in enumerate(banks):
                                    out = proj_bank(p + b)
                                    if bank[0] == "t":
                                        _, tt, c0, cw = bank
                                        ins = token_major(out[:, 0:cw], hT_hi[:, k, tt * P:(tt + 1) * P], hT_lo[:, k, tt * P:(tt + 1) * P],
                                                          wh[:, kk, c0:c0 + cw], wl[:, kk, c0:c0 + cw], k == 0, k == KD - 1)
                                    else:
                                        _, b0, blocks, _, _ = bank
                                        m = GRANK if bank[0] == "g" else P
                                        for blk in range(blocks):
                                            c0 = (b0 + blk) * P
                                            ins = feature_major(out[0:m, blk * T:(blk + 1) * T], hT_hi[:, k, :], hT_lo[:, k, :],
                                                                wh[:, kk, c0:c0 + m], wl[:, kk, c0:c0 + m],
                                                                k == 0 and blk == 0, k == KD - 1)
                            ins.then_inc(w_used, 1)
                    elif name == "z":
                        slab_read(pe, l, "C4")
                        if l == 0:
                            pe.wait_ge(s_small, 64)
                        aux_take(a)
                        for tt in range(TT):
                            ins = plain(aux_bank(a)[:, tt * T:(tt + 1) * T], buf["cg"][0:GRANK + 1, 0, tt * P:(tt + 1) * P],
                                        wg[0:GRANK + 1, l, :])
                        ins.then_inc(aux_done, 1)
                    elif name == "bT":
                        aux_read(pe, FIRST[l, ("z", 0)][2])
                        aux_take(a)
                        for b in range(2):
                            for tt in range(TT):
                                ins = plain(aux_bank(a)[:, b * T + tt * P:b * T + (tt + 1) * P],
                                            gl_g[:, tt, b * P:(b + 1) * P], tri16[:, :])
                        ins.then_inc(aux_done, 1)
                    elif name == "kdT":
                        pe.wait_ge(gla_qk, l + 1)
                        aux_take(a)
                        for b in range(2):
                            for tt in range(TT):
                                ins = pe.transpose(aux_bank(a)[:, tt * T + b * P:tt * T + (b + 1) * P],
                                                   gl_d[:, b, tt * P:(tt + 1) * P], ident[:, :])
                        ins.then_inc(aux_done, 1)
                    elif name == "aT":
                        for par in range(2):
                            rows = slice(64 * par, 64 * par + 64)
                            aux_take(a + par)
                            for j in range(4):
                                tt, b = j // 2, j % 2
                                ins = plain(aux_bank(a + par)[:, j * P:(j + 1) * P], gl_n[rows, b, tt * P:(tt + 1) * P],
                                            buf["cq"][rows, b, tt * P:(tt + 1) * P])
                            ins.then_inc(aux_done, 1)
                    elif name == "u":
                        aux_read(pe, FIRST[l, ("kdT", 0)][2])
                        for s in ("C1", "C2"):
                            slab_read(pe, l, s)
                        for g, cs in enumerate(((0, 2), (1,))):
                            aux_take(a + g)
                            for at, c in enumerate(cs):
                                rows = slice(64 * (c % 2), 64 * (c % 2) + 64)
                                for h in range(GH):
                                    half = slice(64 * (h % 2), 64 * (h % 2) + 64)
                                    col0 = (2 * at + h // 2) * GDV
                                    ins = plain(aux_bank(a + g)[half, col0:col0 + GDV], gl_g[rows, c // 2, h * GDK:(h + 1) * GDK],
                                                buf["cv"][rows, c // 2, h * GDV:(h + 1) * GDV])
                            ins.then_inc(aux_done, 1)
                    elif name == "swap":
                        slab_read(pe, l, "A1")
                        aux_take(a)
                        plain(aux_bank(a)[:, 0:T], swap_m[:, :], buf["ak"][:, 0, :]).then_inc(aux_done, 1)
                    elif name == "oC":
                        for g in range(2):
                            aux_read(pe, FIRST[l, ("aT", 0)][2] + g)
                            aux_read(pe, FIRST[l, ("u", 0)][2] + g)
                        for par in range(2):
                            rows = slice(64 * par, 64 * par + 64)
                            aux_take(a + par)
                            for j in range(4):
                                tt, b = j // 2, j % 2
                                h = 2 * b + par
                                cols = slice(j * GDV, (j + 1) * GDV)
                                plain(aux_bank(a + par)[:, cols], aT[:, par, j, :], buf["cv"][:, tt, h * GDV:(h + 1) * GDV], stop=False)
                                for c in (2 * tt, 2 * tt + 1):
                                    if c:
                                        half = slice(64 * (c % 2), 64 * (c % 2) + 64)
                                        ins = plain(aux_bank(a + par)[half, cols], buf["cq"][rows, b, c * CH:(c + 1) * CH],
                                                    state[rows, c - 1, b, :], start=False)
                            ins.then_inc(aux_done, 1)
                    elif name == "oCT":
                        pe.wait_ge(oc_ready, l + 1)
                        for g in range(2):
                            aux_take(a + g)
                            for hh in range(2):
                                for tt in range(TT):
                                    h = 2 * g + hh
                                    ins = pe.transpose(aux_bank(a + g)[:, hh * T + tt * P:hh * T + (tt + 1) * P],
                                                       oc[:, tt, h * GDV:(h + 1) * GDV], ident[:, :])
                            ins.then_inc(aux_done, 1)
                    elif name[0] == "S":
                        quad = int(name[1])
                        if quad == 0:
                            slab_read(pe, l, "A0")
                            aux_read(pe, FIRST[l, ("swap", 0)][2])
                        if quad == 2:
                            for s in ("B0", "B1", "B2"):
                                slab_read(pe, l, s)
                        for hh in range(4):
                            h = 4 * (quad % 2) + hh
                            rows = slice(64 * (h % 2), 64 * (h % 2) + 64)
                            if quad < 2:
                                q, k = buf["aq"][rows, h // 2, :], buf["ak"][rows, 0 if h // 4 == h % 2 else 1, :]
                            else:
                                q, k = buf["bq"][rows, h // 2, :], buf["bk"][rows, h // 2, :]
                            aux_take(a + hh)
                            plain(aux_bank(a + hh)[:, 0:P], q[:, 0:P], k[:, 0:P])
                            plain(aux_bank(a + hh)[:, P:3 * P], q[:, P:T], k).then_inc(aux_done, 1)
                    elif name[0] == "P":
                        pe.wait_ge(q_prob, 4 * l + int(name[1]) + 1)
                        for hh in range(4):
                            aux_take(a + hh)
                            for blk in range(3):
                                at = (3 * hh + blk) * P
                                sm = xhat[:, :, :].rearrange("p a b -> p (a b)")
                                ins = pe.transpose(aux_bank(a + hh)[:, blk * P:(blk + 1) * P], sm[:, at:at + P], ident[:, :])
                            ins.then_inc(aux_done, 1)
                    elif name[0] == "V":
                        quad = int(name[1])
                        for s in (("A1",) if quad < 2 else ("B2", "B3")):
                            slab_read(pe, l, s)
                        for g in range(4):
                            aux_read(pe, FIRST[l, ("P" + name[1], 0)][2] + g)
                        for g in range(2):
                            aux_take(a + g)
                            for hh in (2 * g, 2 * g + 1):
                                h = 4 * (quad % 2) + hh
                                half = slice(64 * (hh % 2), 64 * (hh % 2) + 64)
                                v = buf["av"][:, :, DH * (h // 4):DH * (h // 4) + DH] if quad < 2 else buf["bv"][:, :, DH * h:DH * (h + 1)]
                                plain(aux_bank(a + g)[half, 0:T], v[:, 0, :], pT[:, hh, 0:T], stop=False)
                                ins = plain(aux_bank(a + g)[half, P:T], v[:, 1, :], pT[:, hh, T:3 * P], start=False)
                            ins.then_inc(aux_done, 1)
                    elif name == "branch":
                        b = i // 3
                        c0, w = WCOLS[i % 3]
                        if i % 3 == 0:
                            for s in (("V0", "V1"), ("V2", "V3"), ("oCT",))[b]:
                                for g in range(2):
                                    aux_read(pe, FIRST[l, (s, 0)][2] + g)
                        for tt in range(TT):
                            proj_take(p + tt)
                        unit_ready(n)
                        wh, wl = unit(n, "hi", 4, w), unit(n, "lo", 4, w)
                        for tt in range(TT):
                            for k in range(4):
                                ins = token_major(proj_bank(p + tt)[:, 0:w], oT_hi[:, b, k, tt * P:(tt + 1) * P],
                                                  oT_lo[:, b, k, tt * P:(tt + 1) * P], wh[:, k, :], wl[:, k, :], k == 0, k == 3)
                        ins.then_inc(w_used, 1)
                    elif name == "yT":
                        pe.wait_ge(y_ready, 12 * (l + 1))
                        rows_T(a, xhat)
                        for g in range(4):
                            aux_read(pe, a + g)
                    elif name in ("wo", "gate", "up"):
                        w = WCOLS[i][1] if name == "wo" else FC
                        for tt in range(TT):
                            proj_take(p + tt)
                        for kh in range(2):
                            unit_ready(n + kh)
                            wh, wl = unit(n + kh, "hi", 4, w), unit(n + kh, "lo", 4, w)
                            for tt in range(TT):
                                for kk in range(4):
                                    k = 4 * kh + kk
                                    ins = token_major(proj_bank(p + tt)[:, 0:w], hT_hi[:, k, tt * P:(tt + 1) * P],
                                                      hT_lo[:, k, tt * P:(tt + 1) * P], wh[:, kk, :], wl[:, kk, :], k == 0, k == KD - 1)
                            ins.then_inc(w_used, 1)
                    elif name == "hT":
                        for tt in range(TT):
                            proj_read(pe, FIRST[l, ("up", i)][1] + tt)
                        for g, (j, m) in enumerate(block_pairs(i)):
                            aux_take(a + g)
                            for b in range(m):
                                for tt in range(TT):
                                    ins = pe.transpose(aux_bank(a + g)[:, b * T + tt * P:b * T + (tt + 1) * P],
                                                       hid[:, tt, (j + b) * P:(j + b + 1) * P], ident[:, :])
                            ins.then_inc(aux_done, 1)
                    elif name == "down":
                        d = FIRST[l, ("down", 0)][1]
                        k0, kn = down_groups(FT)[i]
                        c = min(cc for cc in range(NF) if blocks_done(cc) >= k0 + kn)
                        for g in range(len(block_pairs(c))):
                            aux_read(pe, FIRST[l, ("hT", c)][2] + g)
                        for h in range(2):
                            if i == 0:
                                for tt in range(TT):
                                    proj_take(d + 2 * tt + h)
                            unit_ready(n + h)
                            wh, wl = unit(n + h, "hi", kn, HALF), unit(n + h, "lo", kn, HALF)
                            for tt in range(TT):
                                for kk in range(kn):
                                    k = k0 + kk
                                    ins = token_major(proj_bank(d + 2 * tt + h), hidT_hi[:, k, tt * P:(tt + 1) * P],
                                                      hidT_lo[:, k, tt * P:(tt + 1) * P], wh[:, kk, :], wl[:, kk, :],
                                                      k == 0, k == FT - 1)
                            ins.then_inc(w_used, 1)

            a = ROUTER_AUX
            pe.wait_ge(router_split, 2)
            aux_take(a)
            for tt in range(TT):
                for k in range(KD):
                    ins = token_major(aux_bank(a)[:, tt * NE:(tt + 1) * NE], hT_hi[:, k, tt * P:(tt + 1) * P],
                                      hT_lo[:, k, tt * P:(tt + 1) * P], r_hi[:, k, :], r_lo[:, k, :], k == 0, k == KD - 1)
            ins.then_inc(aux_done, 1)
            pe.wait_ge(picked_ready, 1)
            aux_take(a + 1)
            bank = aux_bank(a + 1)
            plain(bank[:, 0:NE], tri1[:, :], picked[:, 0, :])
            plain(bank[:, NE:2 * NE], tri1[:, :], picked[:, 1, :], stop=False)
            plain(bank[:, NE:2 * NE], ones[:, :], picked[:, 0, :], start=False)
            plain(bank[:, 2 * NE:3 * NE], ones[:, :], picked[:, 0, :], stop=False)
            plain(bank[:, 2 * NE:3 * NE], ones[:, :], picked[:, 1, :], start=False).then_inc(aux_done, 1)

            def gather(a0, src, i=0):
                for part, rows in enumerate((h_hi, h_lo)):
                    for g in range(2):
                        n = a0 + 2 * part + g
                        aux_take(n, i, 2 * E_AUX)
                        for kk in range(4):
                            k = 4 * g + kk
                            for tt in range(TT):
                                ins = plain(aux_bank(n)[:, kk * P:(kk + 1) * P], rows[:, tt, k * P:(k + 1) * P],
                                            sel[:, src, tt, :], start=tt == 0, stop=tt == TT - 1)
                        ins.then_inc(aux_done, 1)

            def scatter(a0, i=0):
                for g in range(4):
                    tt, h = g // 2, g % 2
                    aux_take(a0 + g, i, 2 * E_AUX)
                    lhsT = selT[:, tt * P:(tt + 1) * P]
                    plain(aux_bank(a0 + g), lhsT, y_hi[:, h * HALF:(h + 1) * HALF], stop=False)
                    plain(aux_bank(a0 + g), lhsT, y_lo[:, h * HALF:(h + 1) * HALF], start=False).then_inc(aux_done, 1)

            pe.wait_ge(sel_ready, 1)
            pe.wait_ge(h_ready, 2)
            gather(GATHER_AUX, 0)
            for g in range(4):
                aux_read(pe, GATHER_AUX + g)
            pe.wait_ge(moe_zero, 1)
            pe.wait_ge(route_ready, 1)
            iters = pe.value_load(ids[0:1, 7:8], min_val=NE // 2, max_val=MAXPASS // 2)
            with pe.Fori(0, iters) as i:
                for s in range(2):
                    n0, p0 = UNITS0 + s * E_UNITS, PROJ0 + s * E_PROJ
                    a0 = AUX0 + s * E_AUX

                    def slab(c):
                        for half in range(2):
                            b = p0 + 2 * c + half
                            proj_take(b, i, 2 * E_PROJ)
                            for kh in range(2):
                                n = n0 + 4 * c + 2 * half + kh
                                unit_ready(n, i)
                                wh, wl = unit(n, "hi", 4, FC), unit(n, "lo", 4, FC)
                                for kk in range(4):
                                    k = 4 * kh + kk
                                    ins = token_major(proj_bank(b)[:, 0:FC], xe_hi[:, s, k, :], xe_lo[:, s, k, :],
                                                      wh[:, kk, :], wl[:, kk, :], k == 0, k == KD - 1)
                                ins.then_inc(w_used, 1)

                    def turn(c):
                        a = a0 + 8 + c
                        b0, b1 = (blocks_done(c - 1) if c else 0), blocks_done(c)
                        w = (b1 - b0) * P
                        proj_read(pe, p0 + 2 * c + 1, i, 2 * E_PROJ)
                        aux_take(a, i, 2 * E_AUX)
                        for b in range(b0, b1):
                            ins = pe.transpose(aux_bank(a)[:, (b - b0) * P:(b - b0 + 1) * P], ehid[:, b * P:(b + 1) * P], ident[:, :])
                        if c == 0:
                            for tt in range(TT):
                                ins = pe.transpose(aux_bank(a)[:, w + tt * P:w + (tt + 1) * P], sel[:, s, tt, :].bitcast(F32), ident[:, :])
                        if c == 1:
                            for tt in range(TT):
                                ins = plain(aux_bank(a)[:, w:w + 1], sel[:, s, tt, :].bitcast(F32),
                                            comb[:, tt, bass.ds(i * 2 + s, 1)], start=tt == 0, stop=tt == TT - 1)
                        ins.then_inc(aux_done, 1)

                    def down(g):
                        k0, kn = down_groups(FET)[g]
                        for h in range(2):
                            n, b = n0 + 4 * NFE + 2 * g + h, p0 + 2 * NFE + h
                            if g == 0:
                                proj_take(b, i, 2 * E_PROJ)
                            unit_ready(n, i)
                            wh, wl = unit(n, "hi", kn, HALF), unit(n, "lo", kn, HALF)
                            for kk in range(kn):
                                k = k0 + kk
                                ins = token_major(proj_bank(b), ehT_hi[:, k, :], ehT_lo[:, k, :], wh[:, kk, :], wl[:, kk, :],
                                                  k == 0, k == FET - 1)
                            ins.then_inc(w_used, 1)

                    for g in range(4):
                        aux_read(pe, a0 + 4 - E_AUX + g, i, 2 * E_AUX)
                    slab(0)
                    for h in range(2):
                        proj_read(pe, p0 - 2 + h, i, 2 * E_PROJ)
                    scatter(a0, i)
                    slab(1)
                    pe.wait_ge(sel_ready, s + 2 + i * 2)
                    gather(a0 + 4, (s + 1) % 2, i)
                    slab(2)
                    turn(0)
                    turn(1)
                    slab(3)
                    turn(2)
                    for c in range(2):
                        aux_read(pe, a0 + 8 + c, i, 2 * E_AUX)
                    down(0)
                    turn(3)
                    aux_read(pe, a0 + 10, i, 2 * E_AUX)
                    down(1)
                    aux_read(pe, a0 + 11, i, 2 * E_AUX)
                    down(2)
                    down(3)
            for h in range(2):
                proj_read(pe, PROJ0 - 2 + h, iters, 2 * E_PROJ)
            scatter(AUX0, iters)


_INS = ["x", "norm1_g", "w_in", "swa_sinks", "gla_w_gate", "gla_b_gate", "gla_norm_g", "w_branch_a", "w_branch_b",
        "w_branch_c", "w_o", "norm2_g", "ffn_w_gate", "ffn_w_up", "ffn_w_down", "moe_router", "moe_w_gate",
        "moe_w_up", "moe_w_down", "final_norm_g"]


def kernel(**inputs):
    import numpy as np
    import concourse.bacc as bacc
    from concourse.bass_utils import run_bass_kernel_spmd

    nc = bacc.Bacc("TRN2", target_bir_lowering=False, num_devices=1)
    arrays, tensors = {}, {}
    for name in _INS:
        a = np.ascontiguousarray(inputs[name])
        arrays[f"in_{name}"] = a
        tensors[name] = nc.dram_tensor(f"in_{name}", a.shape, mybir.dt.from_np(a.dtype), kind="ExternalInput").ap()
    tensors["out"] = nc.dram_tensor("out_0", (1, T, D), F32, kind="ExternalOutput").ap()
    build(nc, tensors)
    result = run_bass_kernel_spmd(nc, [arrays], core_ids=[0])
    return result.results[0]["out_0"]
```

```python
from contextlib import ExitStack

import concourse.bass as bass
from concourse import mybir

F32 = mybir.dt.float32
F32R = mybir.dt.float32r
U32 = mybir.dt.uint32
I32 = mybir.dt.int32
ALU = mybir.AluOpType
ACT = mybir.ActivationFunctionType
AX = mybir.AxisListType

P = 128
T, D, LAYERS = 256, 1024, 2
TT = T // P
KD = D // P
DH = 64
SWA_H, SWA_KV, MOBA_H = 8, 2, 8
GH, GDK, GDV, GRANK, CH = 4, 64, 128, 16, 64
BW = 512
F, FE, NE = 2816, 1408, 8
EPS = 1e-6
NEG = -1.0e30

A0, B0, C0, G0 = 0, 768, 2304, 3856
SW = 386
SLABS = {
    "C4": (3840, SW, [("g", 0, 1, "cg", 0), ("t", 0, 16, 370), ("t", 1, 16, 370)]),
    "C0": (C0, 384, [("f", 0, 2, "cq", 0), ("f", 2, 1, "ck", 0)]),
    "C1": (C0 + 384, 384, [("f", 0, 1, "ck", 1), ("t", 0, 128, 256), ("t", 1, 128, 256)]),
    "C2": (C0 + 768, 384, [("t", 0, 0, 384), ("t", 1, 0, 384)]),
    "C3": (C0 + 1152, 384, [("t", 0, 0, 384), ("t", 1, 0, 384)]),
    "A0": (A0, 384, [("f", 0, 2, "aq", 0), ("f", 2, 1, "aq", 2)]),
    "A1": (A0 + 384, 384, [("f", 0, 1, "aq", 3), ("f", 1, 1, "ak", 0), ("t", 0, 256, 128), ("t", 1, 256, 128)]),
    "B0": (B0, 384, [("f", 0, 2, "bq", 0), ("f", 2, 1, "bq", 2)]),
    "B1": (B0 + 384, 384, [("f", 0, 1, "bq", 3), ("f", 1, 2, "bk", 0)]),
    "B2": (B0 + 768, 384, [("f", 0, 2, "bk", 2), ("t", 0, 256, 128), ("t", 1, 256, 128)]),
    "B3": (B0 + 1152, 384, [("t", 0, 0, 384), ("t", 1, 0, 384)]),
}
for _g in range(1, 8):
    SLABS[f"G{_g}"] = (3840 + SW * _g, SW, [("t", 0, 0, SW), ("t", 1, 0, SW)])
GATE0 = SW - GRANK

PIECES = {
    "C4": [(0, GATE0, "gates", 0)],
    "C1": [(0, 256, "cv", 0)],
    "C2": [(0, 256, "cv", 256), (256, 128, "cr", 0)],
    "C3": [(0, 384, "cr", 128)],
    "A1": [(0, 128, "av", 0)],
    "B2": [(0, 128, "bv", 0)],
    "B3": [(0, 384, "bv", 128)],
}
for _g in range(1, 8):
    PIECES[f"G{_g}"] = [(0, SW, "gates", GATE0 + SW * (_g - 1))]

WCOLS = [(0, 352), (352, 352), (704, 320)]
FC = 352
NF, NFE = F // FC, FE // FC
FT, FET = F // P, FE // P
DK = 3
HALF = D // 2


def blocks_done(c):
    return (c + 1) * FC // P


def down_groups(tiles):
    return [(k, min(DK, tiles - k)) for k in range(0, tiles, DK)]


def block_pairs(c):
    a, b = (blocks_done(c - 1) if c else 0), blocks_done(c)
    return [(j, min(2, b - j)) for j in range(a, b, 2)]


def mixer_steps():
    names = ["norm", "C4", "C0", "z", "C1", "bT", "C2", "C3", "kdT", "aT", "A0", "u", "A1", "oC", "swap",
             "B0", "S0", "B1", "B2", "P0", "S1", "V0", "oCT", "B3", "G1", "P1", "S2", "V1", "G2", "G3",
             "P2", "S3", "V2", "G4", "G5", "P3", "G6", "V3", "G7"]
    out = [(n, 0) for n in names]
    out += [("branch", n) for n in range(8)] + [("yT", 0), ("branch", 8), ("yT", 1)]
    return out + [("wo", s) for s in range(3)] + [("norm2", 0)]


def dense_steps():
    out = []
    for c in range(NF):
        out += [("gate", c), ("up", c)]
        if c:
            out.append(("hT", c - 1))
    for g in range(len(down_groups(FT))):
        if g == 3:
            out.append(("hT", NF - 1))
        out.append(("down", g))
    return out


SOFTMAX_IN = {"B1": 0, "B3": 1, "G2": 2, "G4": 3}
URGENT = {("branch", 8): ("yT", 1), ("wo", 2): ("norm2", 0), ("down", len(down_groups(FT)) - 1): ("norm", 0)}
STEPS = {l: mixer_steps() + (dense_steps() if l == 0 else []) for l in range(LAYERS)}


def sizes(step):
    name, i = step
    if name in SLABS:
        return 2, len(SLABS[name][2]), 0, 0
    if name in ("norm", "norm2"):
        return 0, 0, 4, 4
    if name == "yT":
        return 0, 0, 2, 2
    if name in ("z", "bT", "kdT", "swap"):
        return 0, 0, 1, 0
    if name in ("aT", "u", "oC"):
        return 0, 0, 2, 0
    if name == "oCT" or name[0] == "V":
        return 0, 0, 2, 2
    if name[0] in "SP":
        return 0, 0, 4, 0
    if name == "branch":
        return 1, TT, 0, 0
    if name in ("wo", "gate", "up"):
        return 2, TT, 0, 0
    if name == "hT":
        return 0, 0, len(block_pairs(i)), len(block_pairs(i))
    assert name == "down"
    return 2, 2 * TT if i == 0 else 0, 0, 0


FIRST = {}
_at = [0, 0, 0, 0]
for _l in range(LAYERS):
    for _s in STEPS[_l]:
        FIRST[_l, _s] = tuple(_at)
        _at = [a + b for a, b in zip(_at, sizes(_s))]
UNITS0, PROJ0, AUX0, HI0 = _at
ROUTER_AUX = AUX0
GATHER_AUX = AUX0 + 3
AUX0 += 11

NORM_PIECES = [[(0, D)], WCOLS, [(0, HALF), (HALF, HALF)], WCOLS, [(0, HALF), (HALF, HALF)]]


def squares_before(m):
    return sum(TT * len(pieces) for pieces in NORM_PIECES[:m])


def splits_before(l, step):
    n = FIRST[l, step][0] + LEAD
    return () if step in URGENT else range(n, n + sizes(step)[0])


def splits_behind(l, step):
    for urgent, end in URGENT.items():
        n = FIRST[l, step][0] + LEAD
        if step == end and (l, step) not in ((0, ("norm", 0)), (LAYERS - 1, ("norm2", 0))):
            return range(n - sizes(urgent)[0], n)
    return ()


RING, LEAD = 5, 3
E_RING, E_LEAD = 8, 4
CAP = 4 * SW
BANKS = 4

E_UNITS = 2 * 2 * NFE + 2 * len(down_groups(FET))
E_PROJ = 2 * NFE + 2
E_SCATTER = (0, 8)
E_TURN = ((4, 5, 6, 7), (12, 13, 18, 19))
E_GATHER = (14, 20)
E_AUX = 24
E_HI = 4 + 2
MAXPASS = 12
assert 2 * E_UNITS % E_RING == 0 and 2 * E_PROJ % BANKS == 0 and E_AUX % BANKS == 0


def turned(j):
    return {12: (0, 1), 16: (2,), 18: (3,)}.get(j, ())


LAST_UNIT = {}
for _l in range(LAYERS):
    for _s in STEPS[_l]:
        _u, _b, _, _ = sizes(_s)
        _end = FIRST[_l, _s][0] + _u - 1
        if _s == ("down", 0):
            _end = FIRST[_l, ("down", len(down_groups(FT)) - 1)][0] + 1
        for _n in range(_b):
            LAST_UNIT[FIRST[_l, _s][1] + _n] = _end
for _e in range(2):
    _n, _u = PROJ0 + _e * E_PROJ, UNITS0 + _e * E_UNITS
    for _b in range(2 * NFE):
        LAST_UNIT[_n + _b] = _u + 2 * _b + 1
    for _h in range(2):
        LAST_UNIT[_n + 2 * NFE + _h] = _u + E_UNITS - 2 + _h


def uses(n, size, i=0, per=0):
    return n // size + i * (per // size)


def build(nc, t):
    with ExitStack() as ctx:
        scope = [ctx]

        def sb(name, shape, dt=F32):
            return scope[0].enter_context(nc.sbuf_tensor(name, [P] + shape, dt))

        def sem(name):
            return ctx.enter_context(nc.semaphore(name))

        x = sb("x", [TT, D])
        xhat = sb("xhat", [TT, D])
        hT_hi, hT_lo = sb("hT_hi", [KD, T], F32R), sb("hT_lo", [KD, T], F32R)
        def in_one_place(name_a, name_b, shape):
            outer, scope[0] = scope[0], ExitStack()
            a = sb(name_a, shape)
            scope[0].close()
            scope[0] = outer
            return a, sb(name_b, shape, F32R)

        raw, w_lo = in_one_place("raw", "w_lo", [RING, CAP])
        w_hi = sb("w_hi", [RING, CAP], F32R)
        ident, swap_m = sb("ident", [P]), sb("swap_m", [P])
        mask = sb("mask", [2, 3 * P])
        tri16 = sb("tri16", [P])
        tri1, ones = sb("tri1", [P], F32R), sb("ones", [P], F32R)
        iota = sb("iota", [P])
        wg = sb("wg", [LAYERS, GH * GDK])
        normg = sb("normg", [BW])
        gain = sb("gain", [4 * KD])
        sinks = sb("sinks", [LAYERS * SWA_H])
        router, r_split = sb("router", [KD, NE]), sb("r_split", [KD, 2 * NE], F32R)
        fold = sb("fold", [NE])
        nrm = sb("nrm", [8, TT])
        gn = sb("gn", [8, 2 * GH])
        qm, ql, qs = sb("qm", [4, 2]), sb("ql", [4, 2]), sb("qs", [4, 2])

        start = ExitStack()
        scope[0] = start
        iota_i, gain_rows = sb("iota_i", [P], I32), sb("gain_rows", [P])
        tri1_f, ones_f = sb("tri1_f", [P]), sb("ones_f", [P])
        start.close()

        mix = ExitStack()
        scope[0] = mix
        buf = {
            "aq": sb("aq", [4, T]), "ak": sb("ak", [2, T]), "av": sb("av", [TT, P]),
            "bq": sb("bq", [4, T]), "bk": sb("bk", [4, T]), "bv": sb("bv", [TT, BW]),
            "cq": sb("cq", [2, T]), "ck": sb("ck", [2, T]), "cv": sb("cv", [TT, BW]),
            "cr": sb("cr", [TT, BW]), "cg": sb("cg", [1, T]),
        }
        gl_g, gl_b, gl_n, gl_d = sb("gl_g", [TT, T]), sb("gl_b", [2, T]), sb("gl_n", [2, T]), sb("gl_d", [2, T])
        oc = sb("oc", [TT, BW])
        early = ExitStack()
        scope[0] = early
        aT = sb("aT", [2, 4, P])
        state = sb("state", [3, 2, GDV])
        early.close()
        scope[0] = mix
        pT = sb("pT", [4, 3 * P])
        sb("pT_end", [2 * P])
        oT_hi, oT_lo = sb("oT_hi", [3, 4, T], F32R), sb("oT_lo", [3, 4, T], F32R)
        buf["gates"] = sb("gates", [TT, 3 * D])
        mix.close()

        ffn = ExitStack()
        scope[0] = ffn
        hid = sb("hid", [TT, F])
        hidT_hi, hidT_lo = sb("hidT_hi", [FT, T], F32R), sb("hidT_lo", [FT, T], F32R)
        sg = sb("sg", [TT, FC])
        ffn.close()

        moe = ctx
        scope[0] = moe
        raw_e, w_lo_e = in_one_place("raw_e", "w_lo_e", [E_RING - RING, CAP])
        w_hi_e = sb("w_hi_e", [E_RING - RING, CAP], F32R)
        h_hi, h_lo = sb("h_hi", [TT, D], F32R), sb("h_lo", [TT, D], F32R)
        g_row = sb("g_row", [D])
        sel = sb("sel", [TT, 2 * P], F32R)
        selT = sb("selT", [T], F32R)
        xe_hi, xe_lo = sb("xe_hi", [KD, 2 * P], F32R), sb("xe_lo", [KD, 2 * P], F32R)
        comb, slots = sb("comb", [TT, MAXPASS + 2]), sb("slots", [TT, MAXPASS + 2])
        ids = sb("ids", [8], I32)
        esg = sb("esg", [2, FC])
        y_hi, y_lo = sb("y_hi", [D], F32R), sb("y_lo", [D], F32R)
        pslot = sb("pslot", [1])

        routing = ExitStack()
        scope[0] = routing
        lg, oh1, oh2, rt = sb("lg", [TT, NE]), sb("oh1", [TT, NE]), sb("oh2", [TT, NE]), sb("rt", [TT, NE])
        picked = sb("picked", [TT, NE], F32R)
        h_rows = sb("h_rows", [TT, D])
        lgT = sb("lgT", [T])
        ti = sb("ti", [8, TT])
        cnt, over, run1, run2, rank = (sb(n, [NE]) for n in ("cnt", "over", "run1", "run2", "rank"))
        XP = MAXPASS - NE
        oj, ot = sb("oj", [XP, NE]), sb("ot", [XP, NE])
        oslot, ocomb = sb("oslot", [TT, XP, NE]), sb("ocomb", [TT, XP, NE])
        ids_f = sb("ids_f", [8])
        routing.close()
        scope[0] = moe
        ehid = sb("ehid", [FE])
        ehT_hi, ehT_lo = sb("ehT_hi", [FET, P], F32R), sb("ehT_lo", [FET, P], F32R)

        ps = ctx.enter_context(nc.psum_tensor("ps", [P, 2 * BANKS, 512], F32))

        s_x = [sem(f"s_x{tt}") for tt in range(TT)]
        s_gain, s_small = sem("s_gain"), sem("s_small")
        s_normg = sem("s_normg")
        normg_used = sem("normg_used")
        s_grow = sem("s_grow")
        loaded = [sem(f"loaded{i}") for i in range(RING)]
        loaded_e = [sem(f"loaded_e{i}") for i in range(E_RING)]
        hi_done, lo_done, w_used = sem("hi_done"), sem("lo_done"), sem("w_used")
        ident_ready, consts, aT_zero = sem("ident_ready"), sem("consts"), sem("aT_zero")
        pool_seq = sem("pool_seq")
        aux_done = sem("aux_done")
        proj_free = [sem(f"proj_free{i}") for i in range(BANKS)]
        aux_free = [sem(f"aux_free{i}") for i in range(BANKS)]
        part_hi = sem("part_hi")
        dseq, aseq = sem("dseq"), sem("aseq")
        sq_sum, mean_sq, root = sem("sq_sum"), sem("mean_sq"), sem("root")
        xhat_done = sem("xhat_done")
        gain_ready, gain_done = sem("gain_ready"), sem("gain_done")
        z_ln, b_ready, b_exp, gla_qk = sem("z_ln"), sem("b_ready"), sem("b_exp"), sem("gla_qk")
        gn_sum, gn_mean, gn_root, oc_ready = sem("gn_sum"), sem("gn_mean"), sem("gn_root"), sem("oc_ready")
        state_ready = sem("state_ready")
        q_max, q_exp, q_prob = sem("q_max"), sem("q_exp"), sem("q_prob")
        y_ready = sem("y_ready")
        router_split, picked_ready, diff_ready, e_ready = (
            sem("router_split"), sem("picked_ready"), sem("diff_ready"), sem("e_ready"))
        h_ready, h_hi_ready, h_lo_ready = sem("h_ready"), sem("h_hi_ready"), sem("h_lo_ready")
        route_ready = sem("route_ready")
        sel_ready, pslot_ready, moe_zero, x_sum = sem("sel_ready"), sem("pslot_ready"), sem("moe_zero"), sem("x_sum")
        out_ready, s_out = sem("out_ready"), sem("s_out")

        block = ctx.enter_context(nc.Block())

        def slot(n, part, size):
            at = (n - UNITS0) % E_RING
            if n >= UNITS0 and at < E_RING - RING:
                return {"raw": raw_e, "hi": w_hi_e, "lo": w_lo_e}[part][:, at, 0:size]
            at = n % RING if n < UNITS0 else (UNITS0 + at - E_RING) % RING
            return {"raw": raw, "hi": w_hi, "lo": w_lo}[part][:, at, 0:size]

        def unit(n, part, k, w):
            return slot(n, part, k * w).rearrange("p (k c) -> p k c", k=k)

        def load_of(n, i=0):
            if n < UNITS0:
                return loaded[n % RING], 16 * (n // RING + 1)
            m = n - UNITS0
            return loaded_e[m % E_RING], 16 * (m // E_RING + 1 + i * (2 * E_UNITS // E_RING))

        def proj_bank(n):
            return ps[:, n % BANKS, :]

        def aux_bank(n):
            return ps[:, BANKS + n % BANKS, :]

        def projected(eng, n, i=0):
            eng.wait_ge(w_used, LAST_UNIT[n] + 1 + i * 2 * E_UNITS)

        def aux_filled(eng, n, i=0, per=0):
            eng.wait_ge(aux_done, n + 1 + i * per)

        def proj_read(eng, n, i=0, per=0):
            eng.wait_ge(proj_free[n % BANKS], uses(n, BANKS, i, per) + 1)

        def aux_read(eng, n, i=0, per=0):
            eng.wait_ge(aux_free[n % BANKS], uses(n, BANKS, i, per) + 1)

        def slab_read(eng, l, name):
            first = FIRST[l, (name, 0)][1]
            for b in range(len(SLABS[name][2])):
                proj_read(eng, first + b)

        def k_cut(w, k0, k, c0, c):
            return w[k0 * P:(k0 + k) * P, c0:c0 + c].rearrange("(k p) c -> p k c", p=P)

        static_units = []
        for l in range(LAYERS):
            for name, i in STEPS[l]:
                if name in SLABS:
                    c0, w, _ = SLABS[name]
                    static_units += [(k_cut(t["w_in"][l], 4 * kh, 4, c0, w), 4, w) for kh in range(2)]
                elif name == "branch":
                    c0, w = WCOLS[i % 3]
                    static_units.append((k_cut(t["w_branch_" + "abc"[i // 3]][l], 0, 4, c0, w), 4, w))
                elif name == "wo":
                    c0, w = WCOLS[i]
                    static_units += [(k_cut(t["w_o"][l], 4 * kh, 4, c0, w), 4, w) for kh in range(2)]
                elif name in ("gate", "up"):
                    static_units += [(k_cut(t["ffn_w_" + name][l // 2], 4 * kh, 4, FC * i, FC), 4, FC)
                                     for kh in range(2)]
                elif name == "down":
                    k0, k = down_groups(FT)[i]
                    static_units += [(k_cut(t["ffn_w_down"][l // 2], k0, k, HALF * h, HALF), k, HALF)
                                     for h in range(2)]
        assert len(static_units) == UNITS0

        e_units = []
        for c in range(NFE):
            for which in ("gate", "up"):
                e_units += [(which, 4 * kh, 4, FC * c, FC) for kh in range(2)]
        for k0, k in down_groups(FET):
            e_units += [("down", k0, k, HALF * h, HALF) for h in range(2)]
        assert len(e_units) == E_UNITS

        def unit_size(n):
            if n < UNITS0:
                return static_units[n][1] * static_units[n][2]
            _, _, k, _, c = e_units[(n - UNITS0) % E_UNITS]
            return k * c

        @block.sync
        def _(sp):
            for tt in range(TT):
                sp.dma_start(x[:, tt, :], t["x"][0, tt * P:(tt + 1) * P, :]).then_inc(s_x[tt], 16)
            sp.dma_start(gain_rows[0:16, :], t["norm1_g"].rearrange("l (k p) -> (l k) p", p=P)).then_inc(s_gain, 16)
            sp.dma_start(gain_rows[16:32, :], t["norm2_g"].rearrange("l (k p) -> (l k) p", p=P)).then_inc(s_gain, 16)

            def load(n, src, k, w, i=0):
                before = n - (RING if n < UNITS0 else E_RING)
                if before >= 0:
                    sp.wait_ge(w_used, before + 1 + i * 2 * E_UNITS)
                sp.dma_start(unit(n, "raw", k, w), src).then_inc(load_of(n)[0], 16)

            def expert_unit(j, e):
                which, k0, k, c0, c = e_units[j]
                return k_cut(t["moe_w_" + which][0, e], k0, k, c0, c), k, c

            for n, (src, k, w) in enumerate(static_units):
                load(n, src, k, w)
                if n == 1:
                    sp.dma_start(wg[0:GRANK, :, :], t["gla_w_gate"].rearrange("l r c -> r l c")).then_inc(s_small, 16)
                    sp.dma_start(wg[GRANK:GRANK + 1, :, :], t["gla_b_gate"].unsqueeze(0)).then_inc(s_small, 16)
                    sp.dma_start(sinks[:, :], t["swa_sinks"].rearrange("l h -> (l h)").partition_broadcast(P)).then_inc(s_small, 16)
                    sp.dma_start(router[:, :, :], t["moe_router"][0].rearrange("(k p) e -> p k e", p=P)).then_inc(s_small, 16)
                    sp.dma_start(normg[:, :], t["gla_norm_g"][0].partition_broadcast(P)).then_inc(s_normg, 16)
                if n == FIRST[1, ("C4", 0)][0] + 1:
                    sp.wait_ge(normg_used, 1)
                    sp.dma_start(normg[:, :], t["gla_norm_g"][1].partition_broadcast(P)).then_inc(s_normg, 16)
            sp.wait_ge(aux_done, FIRST[1, ("V3", 0)][2] + 2)
            with sp.Fori(0, NE // 2) as i:
                for s in range(2):
                    for j in range(E_UNITS):
                        load(UNITS0 + s * E_UNITS + j, *expert_unit(j, i * 2 + s), i=i)
            sp.wait_ge(route_ready, 1)
            iters = sp.value_load(ids[0:1, 7:8], min_val=NE // 2, max_val=MAXPASS // 2)
            with sp.If(iters > NE // 2):
                with sp.Fori(NE // 2, iters) as i:
                    first = sp.value_load(ids[0:1, bass.ds((i - NE // 2) * 2, 1)], min_val=0, max_val=NE - 1)
                    second = sp.value_load(ids[0:1, bass.ds((i - NE // 2) * 2 + 1, 1)], min_val=0, max_val=NE - 1)
                    for s, e in enumerate((first, second)):
                        for j in range(E_UNITS):
                            load(UNITS0 + s * E_UNITS + j, *expert_unit(j, e), i=i)
            for j in range(E_LEAD):
                load(UNITS0 + j, *expert_unit(j, 0), i=iters)
            for tt in range(TT):
                for h in range(2):
                    cols = slice(h * HALF, (h + 1) * HALF)
                    sp.wait_ge(out_ready, 2 * tt + h + 1)
                    sp.dma_start(t["out"][0, tt * P:(tt + 1) * P, cols], xhat[:, tt, cols]).then_inc(s_out, 16)
            sp.wait_ge(s_out, 16 * 2 * TT)

        @block.gpsimd
        def _(pool):
            seq = [0]

            def link(ins):
                seq[0] += 1
                ins.then_inc(pool_seq, 1)
                pool.wait_ge(pool_seq, seq[0])

            def select(out, op, base, pattern, fill, mult):
                return pool.affine_select(out=out, in_=out, compare_op=op, fill=fill, base=base,
                                          pattern=pattern, channel_multiplier=mult)

            pool.memset(nrm[:, 7, :], 1.0)
            link(pool.memset(ident[:, :], 0.0))
            select(ident[:, :], ALU.not_equal, 0, [[-1, P]], 1.0, 1).then_inc(ident_ready, 1)
            pool.memset(buf["cg"][:, :, :], 1.0)
            pool.memset(swap_m[:, :], 0.0)
            pool.memset(mask[:, :, :], 0.0)
            pool.memset(tri16[:, :], 1.0 / 16.0)
            pool.memset(tri1_f[:, :], 1.0)
            pool.memset(ones_f[:, :], 1.0)
            link(pool.iota(iota_i[:, :], pattern=[[1, P]], base=0, channel_multiplier=0))
            link(select(swap_m[:, 0:64], ALU.not_equal, -64, [[-1, 64]], 1.0, 1))
            link(select(swap_m[:, 64:128], ALU.not_equal, 0, [[-1, 64]], 1.0, 1))
            for b in range(2):
                for blk in (0, 2):
                    link(select(mask[:, b, blk * P:(blk + 1) * P], ALU.is_ge, 0, [[-1, P]], NEG, 1))
            link(select(mask[:, 0, P:2 * P], ALU.is_gt, 0, [[1, P]], NEG, -1))
            link(select(tri1_f[:, :], ALU.is_ge, 0, [[1, P]], 0.0, -1))
            link(select(tri16[:, :], ALU.is_ge, 0, [[1, P]], 0.0, -1))
            link(pool.memset(tri16[0:64, 64:128], 0.0))
            pool.tensor_copy(tri1[:, :], tri1_f[:, :])
            pool.tensor_copy(ones[:, :], ones_f[:, :])
            pool.tensor_copy(iota[:, :], iota_i[:, :])
            pool.wait_ge(ident_ready, 1)
            pool.tensor_tensor(fold[:, :], ident[:, 0:NE], ident[:, NE:2 * NE], ALU.add).then_inc(consts, 1)
            pool.memset(aT[:, :, :, :], 0.0).then_inc(aT_zero, 1)
            pool.wait_ge(w_used, FIRST[1, ("norm", 0)][0])
            pool.memset(buf["cg"][:, :, :], 1.0)
            pool.memset(aT[:, :, :, :], 0.0).then_inc(aT_zero, 1)
            pool.wait_ge(y_ready, 24)
            pool.memset(slots[:, :, :], -1.0)
            pool.memset(comb[:, :, :], 0.0)
            pool.memset(ids_f[:, :], 0.0)
            pool.memset(y_hi[:, :].bitcast(F32), 0.0)
            pool.memset(y_lo[:, :].bitcast(F32), 0.0)
            pool.memset(selT[:, :].bitcast(F32), 0.0).then_inc(moe_zero, 1)
            pool.wait_ge(s_grow, 16)
            pool.wait_ge(xhat_done, 16)
            for tt in range(TT):
                pool.tensor_tensor(h_rows[:, tt, :], xhat[:, tt, :], g_row[:, :], ALU.mult).then_inc(h_ready, 1)

        @block.scalar
        def _(act):
            seq = [0]

            def link(ins):
                seq[0] += 1
                ins.then_inc(aseq, 1)
                act.wait_ge(aseq, seq[0])

            def split_hi(n, i=0):
                k = unit_size(n)
                act.wait_ge(*load_of(n, i))
                act.activation(slot(n, "hi", k), slot(n, "raw", k), ACT.Copy).then_inc(hi_done, 1)

            def squares(piece, tt, m):
                c0, w = NORM_PIECES[m][piece]
                act.activation(xhat[:, tt, c0:c0 + w], x[:, tt, c0:c0 + w], ACT.Square,
                               accum_out=nrm[:, piece, tt:tt + 1]).then_inc(sq_sum, 1)

            def sqrt_table():
                act.activation(nrm[:, 6, :], nrm[:, 7, :], ACT.Sqrt)

            def norm_root(m):
                act.wait_ge(mean_sq, m + 1)
                act.activation(nrm[:, 4, :], nrm[:, 3, :], ACT.Sqrt).then_inc(root, 1)

            def exponentials(l, quad):
                act.wait_ge(q_max, 4 * l + quad + 1)
                sm = xhat[:, :, :].rearrange("p a b -> p (a b)")
                for h in range(4):
                    for tt in range(TT):
                        at, w = 3 * P * h + P * tt, P * (tt + 1)
                        ins = act.activation(sm[:, at:at + w], sm[:, at:at + w], ACT.Exp,
                                             bias=qm[:, h, tt:tt + 1], accum_out=ql[:, h, tt:tt + 1])
                if quad < 2:
                    ins = act.activation(qs[:, :, :], qs[:, :, :], ACT.Exp)
                ins.then_inc(q_exp, 1)

            def wo_squares(l, s):
                for tt in range(TT):
                    proj_read(act, FIRST[l, ("wo", s)][1] + tt)
                    squares(s, tt, 2 * l + 1)

            def gained_hi(l, step, m):
                _, _, a, _ = FIRST[l, step]
                for g in range(4):
                    aux_filled(act, a + g)
                    for kk in range(2):
                        k = 2 * g + kk
                        ins = act.activation(hT_hi[:, k, :], aux_bank(a + g)[:, kk * T:(kk + 1) * T],
                                             ACT.Copy, scale=gain[:, m * KD + k:m * KD + k + 1])
                    ins.then_inc(part_hi, 1)

            for l in range(LAYERS):
                for step in STEPS[l]:
                    name, i = step
                    n, p, a, _ = FIRST[l, step]
                    for u in splits_before(l, step):
                        split_hi(u)
                    if name in SOFTMAX_IN:
                        exponentials(l, SOFTMAX_IN[name])
                    if (name, i) in (("kdT", 0), ("wo", 1), ("down", len(down_groups(FT)) - 1)):
                        sqrt_table()
                    if name == "norm" and l == 0:
                        act.wait_ge(ident_ready, 1)
                        sqrt_table()
                        for tt in range(TT):
                            act.wait_ge(s_x[tt], 16)
                            squares(0, tt, 0)
                        norm_root(0)
                        act.wait_ge(gain_ready, 1)
                        act.activation(gain[:, :], aux_bank(BANKS - 1)[:, 0:4 * KD], ACT.Copy).then_inc(gain_done, 1)
                        split_hi(0)
                        act.wait_ge(gain_done, 1)
                        gained_hi(l, step, l)
                        for u in range(1, LEAD):
                            split_hi(u)
                    elif name == "norm":
                        d = FIRST[0, ("down", 0)][1]
                        for h in range(2):
                            for tt in range(TT):
                                proj_read(act, d + 2 * tt + h)
                                squares(h, tt, 2)
                        norm_root(2)
                        gained_hi(l, step, l)
                    elif name == "norm2":
                        if l == 0:
                            act.wait_ge(s_small, 64)
                            act.activation(r_split[:, :, 0:NE], router[:, :, :], ACT.Copy).then_inc(router_split, 1)
                        else:
                            act.wait_ge(y_ready, 24)
                            act.dma_start(g_row[:, :], t["norm2_g"][1].partition_broadcast(P)).then_inc(s_grow, 16)
                        wo_squares(l, 2)
                        norm_root(2 * l + 1)
                        gained_hi(l, step, 2 + l)
                    elif name in SLABS:
                        for b, bank in enumerate(SLABS[name][2]):
                            if bank[0] != "t":
                                continue
                            projected(act, p + b)
                            tt = bank[1]
                            for c, w, dst, at in PIECES[name]:
                                func = ACT.Silu if dst == "cr" else ACT.Sigmoid if name in ("G4", "G5", "G6", "G7") else ACT.Copy
                                ins = act.activation(buf[dst][:, tt, at:at + w], proj_bank(p + b)[:, c:c + w], func)
                            ins.then_inc(proj_free[(p + b) % BANKS], 1)
                        if name == "G4":
                            slab_read(act, l, "G3")
                            for tt in range(TT):
                                g = buf["gates"][:, tt, 0:GATE0 + 3 * SW]
                                act.activation(g, g, ACT.Sigmoid)
                    elif name == "z":
                        aux_filled(act, a)
                        zb = gl_b[:, :, :].rearrange("p a b -> p (a b)")
                        link(act.activation(zb, aux_bank(a), ACT.Abs))
                        link(act.activation(zb, zb, ACT.Exp, scale=-1.0))
                        act.activation(zb, zb, ACT.Ln, bias=1.0).then_inc(z_ln, 1)
                    elif name == "bT":
                        act.wait_ge(b_ready, l + 1)
                        act.activation(gl_n[:, :, :], gl_b[:, :, :], ACT.Exp, scale=-1.0)
                        act.activation(gl_d[:, :, :], gl_d[:, :, :], ACT.Exp)
                        act.activation(gl_b[:, :, :], gl_b[:, :, :], ACT.Exp).then_inc(b_exp, 1)
                    elif name == "oC":
                        for par in range(2):
                            aux_filled(act, a + par)
                            for j in range(4):
                                ins = act.activation(oc[:, par, j * GDV:(j + 1) * GDV], aux_bank(a + par)[:, j * GDV:(j + 1) * GDV],
                                                     ACT.Square, accum_out=gn[:, 0, 4 * par + j:4 * par + j + 1])
                        ins.then_inc(gn_sum, 1)
                        act.wait_ge(gn_mean, l + 1)
                        act.activation(gn[:, 3, :], gn[:, 1, :], ACT.Sqrt).then_inc(gn_root, 1)
                    elif name[0] == "P":
                        for h in range(4):
                            aux_filled(act, a + h)
                            act.activation(pT[:, h, :], aux_bank(a + h)[:, 0:3 * P], ACT.Copy).then_inc(aux_free[(a + h) % BANKS], 1)
                    elif name[0] == "V" or name == "oCT":
                        br = 2 if name == "oCT" else int(name[1]) // 2
                        for g in range(2):
                            aux_filled(act, a + g)
                            if name == "oCT":
                                out, src = oT_hi[:, 2, 2 * g:2 * g + 2, :], aux_bank(a + g).rearrange("p (a b) -> p a b", a=2)
                            else:
                                out, src = oT_hi[:, br, 2 * (int(name[1]) % 2) + g, :], aux_bank(a + g)[:, 0:T]
                            act.activation(out, src, ACT.Copy).then_inc(part_hi, 1)
                    elif name == "wo" and i:
                        wo_squares(l, i - 1)
                    elif name == "yT":
                        for g in range(2):
                            aux_filled(act, a + g)
                            k = 4 * i + 2 * g
                            act.activation(hT_hi[:, k:k + 2, :], aux_bank(a + g).rearrange("p (a b) -> p a b", a=2),
                                           ACT.Copy).then_inc(part_hi, 1)
                    elif name == "gate":
                        for tt in range(TT):
                            projected(act, p + tt)
                            if i:
                                proj_read(act, FIRST[l, ("up", i - 1)][1] + tt)
                            act.activation(sg[:, tt, :], proj_bank(p + tt)[:, 0:FC], ACT.Silu).then_inc(proj_free[(p + tt) % BANKS], 1)
                    elif name == "hT":
                        for g, (j, m) in enumerate(block_pairs(i)):
                            aux_filled(act, a + g)
                            act.activation(hidT_hi[:, j:j + m, :], aux_bank(a + g)[:, 0:m * T].rearrange("p (a b) -> p a b", a=m),
                                           ACT.Copy).then_inc(part_hi, 1)
                    for u in splits_behind(l, step):
                        split_hi(u)

            aux_filled(act, ROUTER_AUX)
            act.activation(lgT[0:2 * NE, :], aux_bank(ROUTER_AUX)[0:2 * NE, 0:T], ACT.Copy
                           ).then_inc(aux_free[ROUTER_AUX % BANKS], 1)
            for tt in range(TT):
                act.wait_ge(h_ready, tt + 1)
                act.activation(h_hi[:, tt, :], h_rows[:, tt, :], ACT.Copy).then_inc(h_hi_ready, 1)
            act.wait_ge(diff_ready, 1)
            act.activation(ti[:, 5, :], ti[:, 4, :], ACT.Exp).then_inc(e_ready, 1)
            for n in range(LEAD - 2, E_LEAD):
                split_hi(UNITS0 + n)

            def gather_out(a, out, i=0):
                for g in range(4):
                    aux_filled(act, a + g, i, E_AUX)
                    act.activation(out[:, 2 * g:2 * g + 2, :], aux_bank(a + g).rearrange("p (a b) -> p a b", a=2),
                                   ACT.Copy).then_inc(aux_free[(a + g) % BANKS], 1)

            act.dma_start(g_row[:, :], t["final_norm_g"].partition_broadcast(P)).then_inc(s_grow, 16)
            gather_out(GATHER_AUX, xe_hi)
            gather_out(GATHER_AUX + 4, xe_lo)
            act.wait_ge(route_ready, 1)
            iters = act.value_load(ids[0:1, 7:8], min_val=NE // 2, max_val=MAXPASS // 2)
            with act.Fori(0, iters) as i:
                for s in range(2):
                    n0, p0 = UNITS0 + s * E_UNITS, PROJ0 + s * E_PROJ
                    hi0 = HI0 + s * E_HI
                    for j in range(E_UNITS):
                        if (s, j) == (1, 16):
                            gather_out(AUX0 + E_GATHER[0], xe_hi, i)
                        if (s, j) == (1, 20):
                            gather_out(AUX0 + E_GATHER[1], xe_lo, i)
                        for tr in turned(j):
                            a = AUX0 + E_TURN[s][tr]
                            b0, b1 = (blocks_done(tr - 1) if tr else 0), blocks_done(tr)
                            aux_filled(act, a, i, E_AUX)
                            act.activation(ehT_hi[:, b0:b1, :], aux_bank(a)[:, 0:(b1 - b0) * P].rearrange("p (a b) -> p a b", b=P),
                                           ACT.Copy).then_inc(part_hi, 1)
                        if j == E_UNITS - 1:
                            for h in range(2):
                                projected(act, p0 + 2 * NFE + h, i)
                                act.wait_ge(pslot_ready, s + 1 + i * 2)
                                act.activation(y_hi[:, h * HALF:(h + 1) * HALF], proj_bank(p0 + 2 * NFE + h), ACT.Copy,
                                               scale=pslot[:, 0:1]).then_inc(part_hi, 1)
                        split_hi(n0 + j + E_LEAD, i)
                        c = j // 4
                        if j < 4 * NFE and j % 4 == 1:
                            n = p0 + 2 * c
                            projected(act, n, i)
                            proj_read(act, n - 3 if c >= 2 else n + 5 - E_PROJ, i, 2 * E_PROJ)
                            act.activation(esg[:, c % 2, :], proj_bank(n)[:, 0:FC], ACT.Silu).then_inc(proj_free[n % BANKS], 1)

            sqrt_table()
            for g in range(4):
                act.wait_ge(x_sum, g + 1)
                squares(g % 2, g // 2, 4)
            norm_root(4)

        @block.vector
        def _(dve):
            seq = [0]

            def link(ins):
                seq[0] += 1
                ins.then_inc(dseq, 1)
                dve.wait_ge(dseq, seq[0])

            def split_lo(n, i=0):
                k = unit_size(n)
                dve.wait_ge(hi_done, n + 1 + i * 2 * E_UNITS)
                dve.tensor_tensor(slot(n, "lo", k), slot(n, "raw", k), slot(n, "hi", k).bitcast(F32),
                                  ALU.subtract).then_inc(lo_done, 1)

            def part_lo(out, src, hi, number, i=0, scale=1.0):
                dve.wait_ge(part_hi, number + 1 + (i * 2 * E_HI))
                return dve.scalar_tensor_tensor(out=out, in0=src, scalar=scale, in1=hi.bitcast(F32),
                                                op0=ALU.mult, op1=ALU.subtract)

            def rsqrt(y, mean, tmp, roots, count):
                dve.wait_ge(roots, count)
                link(dve.reciprocal(y, y))
                link(dve.scalar_tensor_tensor(out=tmp, in0=y, scalar=-0.5, in1=mean, op0=ALU.mult, op1=ALU.mult))
                link(dve.tensor_tensor(tmp, tmp, y, ALU.mult))
                link(dve.scalar_tensor_tensor(out=y, in0=tmp, scalar=1.5, in1=y, op0=ALU.add, op1=ALU.mult))

            def row_scale(m):
                dve.wait_ge(sq_sum, squares_before(m + 1))
                pieces = len(NORM_PIECES[m])
                if pieces > 1:
                    link(dve.tensor_reduce(nrm[:, 3, :].unsqueeze(2), nrm[:, 0:pieces, :].rearrange("p a b -> p b a"),
                                           AX.X, ALU.add))
                dve.tensor_scalar(nrm[:, 3, :], nrm[:, 3 if pieces > 1 else 0, :], 1.0 / D, EPS, ALU.mult, ALU.add).then_inc(mean_sq, 1)
                dve.wait_ge(mean_sq, m + 1)
                rsqrt(nrm[:, 4, :], nrm[:, 3, :], nrm[:, 5, :], root, m + 1)

            def probabilities(l, quad):
                sm = quad_scores()
                dve.wait_ge(q_exp, 4 * l + quad + 1)
                if quad < 2:
                    link(dve.tensor_tensor(ql[:, :, :], ql[:, :, :], qs[:, :, :], ALU.add))
                link(dve.reciprocal(ql[:, :, :], ql[:, :, :]))
                dve.tensor_tensor(sm[:, :, 0:P], sm[:, :, 0:P], ql[:, :, 0:1].broadcast_to([P, 4, P]), ALU.mult)
                dve.tensor_tensor(sm[:, :, P:3 * P], sm[:, :, P:3 * P], ql[:, :, 1:2].broadcast_to([P, 4, 2 * P]),
                                  ALU.mult).then_inc(q_prob, 1)

            def quad_scores():
                return xhat[:, :, :].rearrange("p a b -> p (a b)")[:, 0:12 * P].rearrange("p (h c) -> p h c", h=4)

            def norm(m):
                row_scale(m)
                for h in range(2):
                    for tt in range(TT):
                        cols = slice(h * HALF, (h + 1) * HALF)
                        dve.tensor_scalar(xhat[:, tt, cols], x[:, tt, cols], nrm[:, 4, tt:tt + 1], None, ALU.mult).then_inc(xhat_done, 1)

            def gained_lo(a, hi0, m):
                if m == 0:
                    dve.wait_ge(gain_done, 1)
                for g in range(4):
                    for kk in range(2):
                        k = 2 * g + kk
                        ins = part_lo(hT_lo[:, k, :], aux_bank(a + g)[:, kk * T:(kk + 1) * T], hT_hi[:, k, :], hi0 + g,
                                      scale=gain[:, m * KD + k:m * KD + k + 1])
                    ins.then_inc(aux_free[(a + g) % BANKS], 1)

            for l in range(LAYERS):
                for step in STEPS[l]:
                    name, i = step
                    n, p, a, hi0 = FIRST[l, step]
                    for u in splits_before(l, step):
                        split_lo(u)
                    if name == "norm":
                        norm(2 * l)
                        if l == 0:
                            split_lo(0)
                        gained_lo(a, hi0, l)
                        if l == 0:
                            for u in range(1, LEAD):
                                split_lo(u)
                            dve.wait_ge(consts, 1)
                        dve.wait_ge(aT_zero, l + 1)
                    elif name == "norm2":
                        if l == 0:
                            dve.wait_ge(router_split, 1)
                            dve.tensor_tensor(r_split[:, :, NE:2 * NE], router[:, :, :], r_split[:, :, 0:NE].bitcast(F32),
                                              ALU.subtract).then_inc(router_split, 1)
                        norm(2 * l + 1)
                        gained_lo(a, hi0, 2 + l)
                    elif name in SLABS:
                        for b, bank in enumerate(SLABS[name][2]):
                            if bank[0] == "t":
                                continue
                            _, _, blocks, dst, at = bank
                            projected(dve, p + b)
                            rows = GRANK if bank[0] == "g" else P
                            dve.tensor_copy(buf[dst][0:rows, at:at + blocks, :],
                                            proj_bank(p + b)[0:rows, 0:blocks * T].rearrange("p (a b) -> p a b", a=blocks)
                                            ).then_inc(proj_free[(p + b) % BANKS], 1)
                        if name == "C3":
                            slab_read(dve, l, "C2")
                            slab_read(dve, l, "C3")
                            dve.wait_ge(s_normg, 16 * (l + 1))
                            dve.tensor_tensor(buf["cr"][:, :, :], buf["cr"][:, :, :],
                                              normg[:, :].unsqueeze(1).broadcast_to([P, TT, BW]), ALU.mult).then_inc(normg_used, 1)
                    elif name == "z":
                        dve.wait_ge(z_ln, l + 1)
                        dve.scalar_tensor_tensor(out=gl_g[:, :, :].rearrange("p a b -> p (a b)"), in0=aux_bank(a), scalar=0.0,
                                                 in1=gl_b[:, :, :].rearrange("p a b -> p (a b)"),
                                                 op0=ALU.min, op1=ALU.subtract).then_inc(aux_free[a % BANKS], 1)
                    elif name == "bT":
                        aux_filled(dve, a)
                        bb = gl_b[:, :, :].rearrange("p a b -> p (a b)")
                        dve.tensor_copy(bb, aux_bank(a)).then_inc(aux_free[a % BANKS], 1)
                        aux_read(dve, a)
                        chunks = bb.rearrange("p (n c) -> p n c", c=CH)
                        dve.tensor_tensor(gl_d[:, :, :].rearrange("p a b -> p (a b)").rearrange("p (n c) -> p n c", c=CH),
                                          chunks[:, :, CH - 1:CH].broadcast_to([P, 2 * T // CH, CH]), chunks,
                                          ALU.subtract).then_inc(b_ready, 1)
                        slab_read(dve, l, "C0")
                        slab_read(dve, l, "C1")
                        dve.wait_ge(b_exp, l + 1)
                        cq, ck = buf["cq"], buf["ck"]

                        def fl(v):
                            return v[:, :, :].rearrange("p a b -> p (a b)")

                        dve.scalar_tensor_tensor(out=fl(cq), in0=fl(cq), scalar=GDK ** -0.5, in1=fl(gl_b), op0=ALU.mult, op1=ALU.mult)
                        dve.tensor_tensor(fl(gl_n), fl(ck), fl(gl_n), ALU.mult)
                        dve.tensor_tensor(fl(gl_d), fl(ck), fl(gl_d), ALU.mult).then_inc(gla_qk, 1)
                    elif name == "kdT":
                        aux_filled(dve, a)
                        dve.tensor_copy(gl_g[:, :, :].rearrange("p a b -> p (a b)"), aux_bank(a)).then_inc(aux_free[a % BANKS], 1)
                    elif name == "aT":
                        for par in range(2):
                            aux_filled(dve, a + par)
                            dve.copy_predicated(aT[:, par, :, :], tri16[:, :].bitcast(U32).unsqueeze(1).broadcast_to([P, 4, P]),
                                                aux_bank(a + par).rearrange("p (a b) -> p a b", a=4)).then_inc(aux_free[(a + par) % BANKS], 1)
                    elif name == "u":
                        for g in range(2):
                            aux_filled(dve, a + g)
                        u02, u1 = aux_bank(a), aux_bank(a + 1)
                        link(dve.tensor_copy(state[:, 0, :, :].rearrange("p a b -> p (a b)"), u02[:, 0:2 * GDV]))
                        for c in (1, 2):
                            src = u1[:, 0:2 * GDV] if c == 1 else u02[:, 2 * GDV:4 * GDV]
                            for b in range(2):
                                ins = dve.scalar_tensor_tensor(out=state[:, c, b, :], in0=state[:, c - 1, b, :],
                                                               scalar=gl_b[:, b, (c + 1) * CH - 1:(c + 1) * CH],
                                                               in1=src[:, b * GDV:(b + 1) * GDV], op0=ALU.mult, op1=ALU.add)
                                if b == 0:
                                    link(ins)
                            ins.then_inc(aux_free[(a + 2 - c) % BANKS], 1)
                            aux_read(dve, a + 2 - c)
                    elif name == "swap":
                        aux_filled(dve, a)
                        dve.tensor_copy(buf["ak"][:, 1, :], aux_bank(a)[:, 0:T]).then_inc(aux_free[a % BANKS], 1)
                    elif name == "oC":
                        dve.wait_ge(gn_sum, l + 1)
                        dve.tensor_scalar(gn[:, 1, :], gn[:, 0, :], 1.0 / GDV, EPS, ALU.mult, ALU.add).then_inc(gn_mean, 1)
                        dve.wait_ge(gn_mean, l + 1)
                        rsqrt(gn[:, 3, :], gn[:, 1, :], gn[:, 2, :], gn_root, l + 1)
                        for par in range(2):
                            out = oc[:, :, :].rearrange("p t (b q d) -> p (t b) q d", b=2, q=2)[:, :, par, :]
                            dve.tensor_tensor(out, aux_bank(a + par).rearrange("p (j d) -> p j d", j=4),
                                              gn[:, 3, 4 * par:4 * par + 4].unsqueeze(2).broadcast_to([P, 4, GDV]),
                                              ALU.mult).then_inc(aux_free[(a + par) % BANKS], 1)
                            aux_read(dve, a + par)
                        dve.tensor_tensor(oc[:, :, :], oc[:, :, :], buf["cr"][:, :, :], ALU.mult).then_inc(oc_ready, 1)
                    elif name[0] == "S":
                        quad = int(name[1])
                        q = 4 * l + quad
                        sm = quad_scores()
                        for h in range(4):
                            aux_filled(dve, a + h)
                            dve.scalar_tensor_tensor(out=sm[:, h, :], in0=aux_bank(a + h)[:, 0:3 * P], scalar=DH ** -0.5,
                                                     in1=mask[:, quad // 2, :], op0=ALU.mult, op1=ALU.add
                                                     ).then_inc(aux_free[(a + h) % BANKS], 1)
                        aux_read(dve, a + 3)
                        dve.tensor_reduce(qm[:, :, 0:1], sm[:, :, 0:P], AX.X, ALU.max)
                        link(dve.tensor_reduce(qm[:, :, 1:2], sm[:, :, P:3 * P], AX.X, ALU.max))
                        if quad < 2:
                            if q == 0:
                                dve.wait_ge(s_small, 64)
                            s0 = SWA_H * l + 4 * quad
                            sk = sinks[:, s0:s0 + 4].unsqueeze(2).broadcast_to([P, 4, 2])
                            link(dve.tensor_tensor(qm[:, :, :], qm[:, :, :], sk, ALU.max))
                            link(dve.tensor_scalar(qm[:, :, :], qm[:, :, :], -1.0, None, ALU.mult))
                            dve.tensor_tensor(qs[:, :, :], qm[:, :, :], sk, ALU.add).then_inc(q_max, 1)
                        else:
                            dve.tensor_scalar(qm[:, :, :], qm[:, :, :], -1.0, None, ALU.mult).then_inc(q_max, 1)
                    elif name[0] == "V" or name == "oCT":
                        for g in range(2):
                            if name == "oCT":
                                out, hi = oT_lo[:, 2, 2 * g:2 * g + 2, :], oT_hi[:, 2, 2 * g:2 * g + 2, :]
                                src = aux_bank(a + g).rearrange("p (a b) -> p a b", a=2)
                            else:
                                br, k = int(name[1]) // 2, 2 * (int(name[1]) % 2) + g
                                out, hi, src = oT_lo[:, br, k, :], oT_hi[:, br, k, :], aux_bank(a + g)[:, 0:T]
                            part_lo(out, src, hi, hi0 + g).then_inc(aux_free[(a + g) % BANKS], 1)
                    elif name == "branch":
                        b, s = i // 3, i % 3
                        c0, w = WCOLS[s]
                        if i == 0:
                            slab_read(dve, l, "G7")
                        for tt in range(TT):
                            projected(dve, p + tt)
                            gate = buf["gates"][:, tt, b * D + c0:b * D + c0 + w]
                            out = xhat[:, tt, c0:c0 + w]
                            tmp = pT[:, 2 * tt:2 * tt + 2, :].rearrange("p a b -> p (a b)")[:, 0:w]
                            dve.tensor_tensor(out if b == 0 else tmp, proj_bank(p + tt)[:, 0:w], gate,
                                              ALU.mult).then_inc(proj_free[(p + tt) % BANKS], 1)
                            if b:
                                proj_read(dve, p + tt)
                                dve.tensor_tensor(out, out, tmp, ALU.add).then_inc(y_ready, 1)
                    elif name == "yT":
                        for g in range(2):
                            k = 4 * i + 2 * g
                            part_lo(hT_lo[:, k:k + 2, :], aux_bank(a + g).rearrange("p (a b) -> p a b", a=2),
                                    hT_hi[:, k:k + 2, :], hi0 + g).then_inc(aux_free[(a + g) % BANKS], 1)
                    elif name == "wo":
                        c0, w = WCOLS[i]
                        for tt in range(TT):
                            projected(dve, p + tt)
                            dve.tensor_tensor(x[:, tt, c0:c0 + w], proj_bank(p + tt)[:, 0:w], x[:, tt, c0:c0 + w],
                                              ALU.add).then_inc(proj_free[(p + tt) % BANKS], 1)
                    elif name == "up":
                        for tt in range(TT):
                            proj_read(dve, FIRST[l, ("gate", i)][1] + tt)
                            projected(dve, p + tt)
                            dve.tensor_tensor(hid[:, tt, FC * i:FC * (i + 1)], proj_bank(p + tt)[:, 0:FC], sg[:, tt, :],
                                              ALU.mult).then_inc(proj_free[(p + tt) % BANKS], 1)
                    elif name == "hT":
                        for g, (j, m) in enumerate(block_pairs(i)):
                            part_lo(hidT_lo[:, j:j + m, :], aux_bank(a + g)[:, 0:m * T].rearrange("p (a b) -> p a b", a=m),
                                    hidT_hi[:, j:j + m, :], hi0 + g).then_inc(aux_free[(a + g) % BANKS], 1)
                    elif name == "down" and i == len(down_groups(FT)) - 1:
                        d = FIRST[l, ("down", 0)][1]
                        for h in range(2):
                            for tt in range(TT):
                                projected(dve, d + 2 * tt + h)
                                dve.tensor_tensor(x[:, tt, h * HALF:(h + 1) * HALF], proj_bank(d + 2 * tt + h),
                                                  x[:, tt, h * HALF:(h + 1) * HALF],
                                                  ALU.add).then_inc(proj_free[(d + 2 * tt + h) % BANKS], 1)
                    if name in SOFTMAX_IN:
                        probabilities(l, SOFTMAX_IN[name])
                    for u in splits_behind(l, step):
                        split_lo(u)

            a = ROUTER_AUX + 1
            aux_filled(dve, a)
            dve.tensor_copy(lg[:, :, :], aux_bank(a)[:, 0:TT * NE].rearrange("p (a b) -> p a b", a=TT)
                            ).then_inc(aux_free[a % BANKS], 1)
            aux_read(dve, a)

            ids8 = iota[:, 0:NE].unsqueeze(1).broadcast_to([P, TT, NE])

            def col(v):
                return v.unsqueeze(2).broadcast_to([P, TT, NE])

            def first_max(logits, top, onehot):
                link(dve.tensor_reduce(ti[:, top, :].unsqueeze(2), logits, AX.X, ALU.max))
                link(dve.tensor_tensor(rt[:, :, :], logits, col(ti[:, top, :]), ALU.is_equal))
                link(dve.tensor_scalar(rt[:, :, :], rt[:, :, :], -float(NE), float(NE), ALU.mult, ALU.add))
                link(dve.tensor_tensor(rt[:, :, :], rt[:, :, :], ids8, ALU.add))
                link(dve.tensor_reduce(ti[:, 2, :].unsqueeze(2), rt[:, :, :], AX.X, ALU.min))
                link(dve.tensor_tensor(onehot, ids8, col(ti[:, 2, :]), ALU.is_equal))

            first_max(lg[:, :, :], 0, oh1[:, :, :])
            link(dve.scalar_tensor_tensor(out=lg[:, :, :], in0=oh1[:, :, :], scalar=-3.0e38, in1=lg[:, :, :],
                                          op0=ALU.mult, op1=ALU.add))
            first_max(lg[:, :, :], 1, oh2[:, :, :])
            dve.tensor_tensor(picked[:, :, :], oh1[:, :, :], oh2[:, :, :], ALU.add).then_inc(picked_ready, 1)
            dve.tensor_tensor(ti[:, 4, :], ti[:, 1, :], ti[:, 0, :], ALU.subtract).then_inc(diff_ready, 1)

            def h_rest(tt):
                dve.wait_ge(h_hi_ready, tt + 1)
                dve.tensor_tensor(h_lo[:, tt, :], h_rows[:, tt, :], h_hi[:, tt, :].bitcast(F32), ALU.subtract).then_inc(h_lo_ready, 1)

            h_rest(0)
            aux_filled(dve, a + 1)
            link(dve.tensor_tensor(rt[:, :, :], aux_bank(a + 1)[:, 0:TT * NE].rearrange("p (a b) -> p a b", a=TT),
                                   picked[:, :, :].bitcast(F32), ALU.mult))
            dve.tensor_copy(cnt[:, :], aux_bank(a + 1)[:, TT * NE:(TT + 1) * NE]).then_inc(aux_free[(a + 1) % BANKS], 1)
            aux_read(dve, a + 1)
            dve.wait_ge(moe_zero, 1)
            link(dve.tensor_scalar(slots[:, :, 0:NE], rt[:, :, :], -1.0, None, ALU.add))

            def select(columns):
                for dst, column in enumerate(columns):
                    for tt in range(TT):
                        ins = dve.tensor_scalar(sel[:, tt, dst * P:(dst + 1) * P], iota[:, :], slots[:, tt, column], None, ALU.is_equal)
                ins.then_inc(sel_ready, 1)

            select((slice(0, 1), slice(1, 2)))
            h_rest(1)
            dve.wait_ge(e_ready, 1)
            link(dve.tensor_scalar(ti[:, 6, :], ti[:, 5, :], 1.0, None, ALU.add))
            link(dve.reciprocal(ti[:, 6, :], ti[:, 6, :]))
            link(dve.tensor_tensor(ti[:, 7, :], ti[:, 5, :], ti[:, 6, :], ALU.mult))
            dve.tensor_tensor(oh1[:, :, :], oh1[:, :, :], col(ti[:, 6, :]), ALU.mult)
            link(dve.tensor_tensor(oh2[:, :, :], oh2[:, :, :], col(ti[:, 7, :]), ALU.mult))
            dve.tensor_tensor(comb[:, :, 0:NE], oh1[:, :, :], oh2[:, :, :], ALU.add)
            link(dve.tensor_scalar(over[:, :], cnt[:, :], float(P), None, ALU.is_gt))
            for src, dst, shift in ((over, run1, 1), (run1, run2, 2), (run2, rank, 4)):
                dve.tensor_copy(dst[:, 0:shift], src[:, 0:shift])
                link(dve.tensor_tensor(dst[:, shift:NE], src[:, shift:NE], src[:, 0:NE - shift], ALU.add))
            link(dve.tensor_tensor(rank[:, :], rank[:, :], over[:, :], ALU.mult))
            link(dve.tensor_tensor(oj[:, :, :], rank[:, :].unsqueeze(1).broadcast_to([P, XP, NE]),
                                   iota[:, 1:XP + 1].unsqueeze(2).broadcast_to([P, XP, NE]), ALU.is_equal))
            ojt = oj[:, :, :].unsqueeze(1).broadcast_to([P, TT, XP, NE])
            dve.tensor_tensor(ot[:, :, :], oj[:, :, :], iota[:, 0:NE].unsqueeze(1).broadcast_to([P, XP, NE]), ALU.mult)
            dve.tensor_tensor(oslot[:, :, :, :], slots[:, :, 0:NE].unsqueeze(2).broadcast_to([P, TT, XP, NE]), ojt, ALU.mult)
            dve.tensor_reduce(ids_f[:, 5:6], rank[:, :], AX.X, ALU.max)
            link(dve.tensor_tensor(ocomb[:, :, :, :], comb[:, :, 0:NE].unsqueeze(2).broadcast_to([P, TT, XP, NE]), ojt, ALU.mult))
            dve.tensor_scalar(ids_f[:, 6:7], ids_f[:, 5:6], 0.0, float(NE // 2), ALU.is_gt, ALU.add)
            dve.tensor_scalar(ids_f[:, 7:8], ids_f[:, 5:6], 2.0, None, ALU.is_gt)
            dve.tensor_reduce(ids_f[:, 0:XP], ot[:, :, :], AX.X, ALU.add)
            dve.tensor_reduce(slots[:, :, NE:NE + XP], oslot[:, :, :, :], AX.X, ALU.add)
            link(dve.tensor_reduce(comb[:, :, NE:NE + XP], ocomb[:, :, :, :], AX.X, ALU.add))
            dve.tensor_scalar(slots[:, :, NE:NE + XP], slots[:, :, NE:NE + XP], -float(P), None, ALU.add)
            link(dve.tensor_tensor(ids_f[:, 7:8], ids_f[:, 7:8], ids_f[:, 6:7], ALU.add))
            dve.tensor_copy(ids[:, :], ids_f[:, :]).then_inc(route_ready, 1)
            dve.wait_ge(route_ready, 1)
            for n in range(LEAD - 2, E_LEAD):
                split_lo(UNITS0 + n)
            iters = dve.value_load(ids[0:1, 7:8], min_val=NE // 2, max_val=MAXPASS // 2)

            with dve.Fori(0, iters) as i:
                for s in range(2):
                    n0, p0 = UNITS0 + s * E_UNITS, PROJ0 + s * E_PROJ
                    hi0 = HI0 + s * E_HI
                    for j in range(E_UNITS):
                        if j == 4:
                            for g in range(4):
                                tt, h = g // 2, g % 2
                                a = AUX0 + E_SCATTER[s] + g
                                aux_filled(dve, a, i, E_AUX)
                                xs = x[:, tt, h * HALF:(h + 1) * HALF]
                                dve.tensor_tensor(xs, aux_bank(a), xs, ALU.add).then_inc(aux_free[a % BANKS], 1)
                        for tr in turned(j):
                            a = AUX0 + E_TURN[s][tr]
                            b0, b1 = (blocks_done(tr - 1) if tr else 0), blocks_done(tr)
                            w = (b1 - b0) * P
                            aux_filled(dve, a, i, E_AUX)
                            dve.wait_ge(part_hi, hi0 + tr + 1 + i * 2 * E_HI)
                            if tr == 0:
                                dve.tensor_copy(selT[:, :], aux_bank(a)[:, w:w + T])
                            if tr == 1:
                                dve.tensor_copy(pslot[:, :], aux_bank(a)[:, w:w + 1]).then_inc(pslot_ready, 1)
                            part_lo(ehT_lo[:, b0:b1, :], aux_bank(a)[:, 0:w].rearrange("p (a b) -> p a b", b=P),
                                    ehT_hi[:, b0:b1, :], hi0 + tr, i).then_inc(aux_free[a % BANKS], 1)
                        if (s, j) == (1, 12):
                            select([bass.ds(i * 2 + 2 + d, 1) for d in range(2)])
                        if j == E_UNITS - 1:
                            for h in range(2):
                                n = p0 + 2 * NFE + h
                                dve.wait_ge(pslot_ready, s + 1 + i * 2)
                                part_lo(y_lo[:, h * HALF:(h + 1) * HALF], proj_bank(n), y_hi[:, h * HALF:(h + 1) * HALF],
                                        hi0 + 4 + h, i, scale=pslot[:, 0:1]).then_inc(proj_free[n % BANKS], 1)
                        split_lo(n0 + j + E_LEAD, i)
                        c = j // 4
                        if j < 4 * NFE and j % 4 == 3:
                            n = p0 + 2 * c + 1
                            proj_read(dve, n - 1, i, 2 * E_PROJ)
                            projected(dve, n, i)
                            dve.tensor_tensor(ehid[:, FC * c:FC * (c + 1)], proj_bank(n)[:, 0:FC], esg[:, c % 2, :],
                                              ALU.mult).then_inc(proj_free[n % BANKS], 1)

            for g in range(4):
                tt, h = g // 2, g % 2
                aux_filled(dve, AUX0 + g, iters, E_AUX)
                xs = x[:, tt, h * HALF:(h + 1) * HALF]
                dve.tensor_tensor(xs, aux_bank(AUX0 + g), xs, ALU.add).then_inc(x_sum, 1)

            row_scale(4)
            dve.wait_ge(s_grow, 32)
            for tt in range(TT):
                for h in range(2):
                    cols = slice(h * HALF, (h + 1) * HALF)
                    dve.scalar_tensor_tensor(out=xhat[:, tt, cols], in0=x[:, tt, cols], scalar=nrm[:, 4, tt:tt + 1],
                                             in1=g_row[:, cols], op0=ALU.mult, op1=ALU.mult).then_inc(out_ready, 1)

        @block.tensor
        def _(pe):
            def proj_take(n, i=0, per=0):
                if n >= BANKS:
                    pe.wait_ge(proj_free[n % BANKS], uses(n, BANKS, i, per))

            def aux_take(n, i=0, per=0):
                if n >= BANKS:
                    pe.wait_ge(aux_free[n % BANKS], uses(n, BANKS, i, per))

            def unit_ready(n, i=0):
                pe.wait_ge(lo_done, n + 1 + i * 2 * E_UNITS)

            def token_major(out, hi, lo, wh, wl, first, last):
                pe.matmul(out, hi, wh, start=first, stop=False, skip_group_check=True)
                pe.matmul(out, hi, wl, start=False, stop=False, skip_group_check=True)
                return pe.matmul(out, lo, wh, start=False, stop=last, skip_group_check=True)

            def feature_major(out, hi, lo, wh, wl, first, last):
                pe.matmul(out, wh, hi, start=first, stop=False, skip_group_check=True)
                pe.matmul(out, wh, lo, start=False, stop=False, skip_group_check=True)
                return pe.matmul(out, wl, hi, start=False, stop=last, skip_group_check=True)

            def plain(out, lhsT, rhs, start=True, stop=True):
                return pe.matmul(out, lhsT, rhs, start=start, stop=stop, skip_group_check=True)

            def rows_T(a, src, banks, k0=0):
                for g in range(banks):
                    aux_take(a + g)
                    for kk in range(2):
                        k = k0 + 2 * g + kk
                        for tt in range(TT):
                            ins = pe.transpose(aux_bank(a + g)[:, kk * T + tt * P:kk * T + (tt + 1) * P],
                                               src[:, tt, k * P:(k + 1) * P], ident[:, :])
                    ins.then_inc(aux_done, 1)

            hT_banks = {}

            def hT_ready(kh):
                for n in hT_banks.pop(kh, ()):
                    aux_read(pe, n)

            pe.wait_ge(ident_ready, 1)
            pe.wait_ge(s_gain, 32)
            pe.transpose(aux_bank(BANKS - 1)[:, 0:4 * KD], gain_rows[0:4 * KD, :], ident[0:4 * KD, 0:4 * KD]).then_inc(gain_ready, 1)
            for l in range(LAYERS):
                for step in STEPS[l]:
                    name, i = step
                    n, p, a, _ = FIRST[l, step]
                    if name in ("norm", "norm2"):
                        if l == 0 and name == "norm":
                            pe.wait_ge(gain_done, 1)
                        for h in range(2):
                            pe.wait_ge(xhat_done, 4 * (2 * l + (name == "norm2")) + 2 * h + 2)
                            rows_T(a + 2 * h, xhat, 2, 4 * h)
                            hT_banks[h] = (a + 2 * h, a + 2 * h + 1)
                    elif name in SLABS:
                        _, w, banks = SLABS[name]
                        for b in range(len(banks)):
                            proj_take(p + b)
                        for kh in range(2):
                            hT_ready(kh)
                            unit_ready(n + kh)
                            wh, wl = unit(n + kh, "hi", 4, w), unit(n + kh, "lo", 4, w)
                            for kk in range(4):
                                k = 4 * kh + kk
                                for b, bank in enumerate(banks):
                                    out = proj_bank(p + b)
                                    if bank[0] == "t":
                                        _, tt, c0, cw = bank
                                        ins = token_major(out[:, 0:cw], hT_hi[:, k, tt * P:(tt + 1) * P], hT_lo[:, k, tt * P:(tt + 1) * P],
                                                          wh[:, kk, c0:c0 + cw], wl[:, kk, c0:c0 + cw], k == 0, k == KD - 1)
                                    else:
                                        _, b0, blocks, _, _ = bank
                                        m = GRANK if bank[0] == "g" else P
                                        for blk in range(blocks):
                                            c0 = (b0 + blk) * P
                                            ins = feature_major(out[0:m, blk * T:(blk + 1) * T], hT_hi[:, k, :], hT_lo[:, k, :],
                                                                wh[:, kk, c0:c0 + m], wl[:, kk, c0:c0 + m],
                                                                k == 0 and blk == 0, k == KD - 1)
                            ins.then_inc(w_used, 1)
                    elif name == "z":
                        slab_read(pe, l, "C4")
                        if l == 0:
                            pe.wait_ge(s_small, 64)
                            pe.wait_ge(consts, 1)
                        aux_take(a)
                        for tt in range(TT):
                            ins = plain(aux_bank(a)[:, tt * T:(tt + 1) * T], buf["cg"][0:GRANK + 1, 0, tt * P:(tt + 1) * P],
                                        wg[0:GRANK + 1, l, :])
                        ins.then_inc(aux_done, 1)
                    elif name == "bT":
                        aux_read(pe, FIRST[l, ("z", 0)][2])
                        aux_take(a)
                        for b in range(2):
                            for tt in range(TT):
                                ins = plain(aux_bank(a)[:, b * T + tt * P:b * T + (tt + 1) * P],
                                            gl_g[:, tt, b * P:(b + 1) * P], tri16[:, :])
                        ins.then_inc(aux_done, 1)
                    elif name == "kdT":
                        pe.wait_ge(gla_qk, l + 1)
                        aux_take(a)
                        for b in range(2):
                            for tt in range(TT):
                                ins = pe.transpose(aux_bank(a)[:, tt * T + b * P:tt * T + (b + 1) * P],
                                                   gl_d[:, b, tt * P:(tt + 1) * P], ident[:, :])
                        ins.then_inc(aux_done, 1)
                    elif name == "aT":
                        for par in range(2):
                            rows = slice(64 * par, 64 * par + 64)
                            aux_take(a + par)
                            for j in range(4):
                                tt, b = j // 2, j % 2
                                ins = plain(aux_bank(a + par)[:, j * P:(j + 1) * P], gl_n[rows, b, tt * P:(tt + 1) * P],
                                            buf["cq"][rows, b, tt * P:(tt + 1) * P])
                            ins.then_inc(aux_done, 1)
                    elif name == "u":
                        aux_read(pe, FIRST[l, ("kdT", 0)][2])
                        for s in ("C1", "C2"):
                            slab_read(pe, l, s)
                        for g, cs in enumerate(((0, 2), (1,))):
                            aux_take(a + g)
                            for at, c in enumerate(cs):
                                rows = slice(64 * (c % 2), 64 * (c % 2) + 64)
                                for h in range(GH):
                                    half = slice(64 * (h % 2), 64 * (h % 2) + 64)
                                    col0 = (2 * at + h // 2) * GDV
                                    ins = plain(aux_bank(a + g)[half, col0:col0 + GDV], gl_g[rows, c // 2, h * GDK:(h + 1) * GDK],
                                                buf["cv"][rows, c // 2, h * GDV:(h + 1) * GDV])
                            ins.then_inc(aux_done, 1)
                    elif name == "swap":
                        slab_read(pe, l, "A1")
                        aux_take(a)
                        plain(aux_bank(a)[:, 0:T], swap_m[:, :], buf["ak"][:, 0, :]).then_inc(aux_done, 1)
                    elif name == "oC":
                        for g in range(2):
                            aux_read(pe, FIRST[l, ("aT", 0)][2] + g)
                            aux_read(pe, FIRST[l, ("u", 0)][2] + g)
                        for par in range(2):
                            rows = slice(64 * par, 64 * par + 64)
                            aux_take(a + par)
                            for j in range(4):
                                tt, b = j // 2, j % 2
                                h = 2 * b + par
                                cols = slice(j * GDV, (j + 1) * GDV)
                                plain(aux_bank(a + par)[:, cols], aT[:, par, j, :], buf["cv"][:, tt, h * GDV:(h + 1) * GDV], stop=False)
                                for c in (2 * tt, 2 * tt + 1):
                                    if c:
                                        half = slice(64 * (c % 2), 64 * (c % 2) + 64)
                                        ins = plain(aux_bank(a + par)[half, cols], buf["cq"][rows, b, c * CH:(c + 1) * CH],
                                                    state[rows, c - 1, b, :], start=False)
                            ins.then_inc(aux_done, 1)
                    elif name == "oCT":
                        pe.wait_ge(oc_ready, l + 1)
                        for g in range(2):
                            aux_take(a + g)
                            for hh in range(2):
                                for tt in range(TT):
                                    h = 2 * g + hh
                                    ins = pe.transpose(aux_bank(a + g)[:, hh * T + tt * P:hh * T + (tt + 1) * P],
                                                       oc[:, tt, h * GDV:(h + 1) * GDV], ident[:, :])
                            ins.then_inc(aux_done, 1)
                    elif name[0] == "S":
                        quad = int(name[1])
                        if quad == 0:
                            slab_read(pe, l, "A0")
                            aux_read(pe, FIRST[l, ("swap", 0)][2])
                        if quad == 2:
                            for s in ("B0", "B1", "B2"):
                                slab_read(pe, l, s)
                        for hh in range(4):
                            h = 4 * (quad % 2) + hh
                            rows = slice(64 * (h % 2), 64 * (h % 2) + 64)
                            if quad < 2:
                                q, k = buf["aq"][rows, h // 2, :], buf["ak"][rows, 0 if h // 4 == h % 2 else 1, :]
                            else:
                                q, k = buf["bq"][rows, h // 2, :], buf["bk"][rows, h // 2, :]
                            aux_take(a + hh)
                            plain(aux_bank(a + hh)[:, 0:P], q[:, 0:P], k[:, 0:P])
                            plain(aux_bank(a + hh)[:, P:3 * P], q[:, P:T], k).then_inc(aux_done, 1)
                    elif name[0] == "P":
                        pe.wait_ge(q_prob, 4 * l + int(name[1]) + 1)
                        for hh in range(4):
                            aux_take(a + hh)
                            for blk in range(3):
                                at = (3 * hh + blk) * P
                                sm = xhat[:, :, :].rearrange("p a b -> p (a b)")
                                ins = pe.transpose(aux_bank(a + hh)[:, blk * P:(blk + 1) * P], sm[:, at:at + P], ident[:, :])
                            ins.then_inc(aux_done, 1)
                    elif name[0] == "V":
                        quad = int(name[1])
                        for s in (("A1",) if quad < 2 else ("B2", "B3")):
                            slab_read(pe, l, s)
                        for g in range(4):
                            aux_read(pe, FIRST[l, ("P" + name[1], 0)][2] + g)
                        for g in range(2):
                            aux_take(a + g)
                            for hh in (2 * g, 2 * g + 1):
                                h = 4 * (quad % 2) + hh
                                half = slice(64 * (hh % 2), 64 * (hh % 2) + 64)
                                v = buf["av"][:, :, DH * (h // 4):DH * (h // 4) + DH] if quad < 2 else buf["bv"][:, :, DH * h:DH * (h + 1)]
                                plain(aux_bank(a + g)[half, 0:T], v[:, 0, :], pT[:, hh, 0:T], stop=False)
                                ins = plain(aux_bank(a + g)[half, P:T], v[:, 1, :], pT[:, hh, T:3 * P], start=False)
                            ins.then_inc(aux_done, 1)
                    elif name == "branch":
                        b = i // 3
                        c0, w = WCOLS[i % 3]
                        if i % 3 == 0:
                            for s in (("V0", "V1"), ("V2", "V3"), ("oCT",))[b]:
                                for g in range(2):
                                    aux_read(pe, FIRST[l, (s, 0)][2] + g)
                        for tt in range(TT):
                            proj_take(p + tt)
                        unit_ready(n)
                        wh, wl = unit(n, "hi", 4, w), unit(n, "lo", 4, w)
                        for tt in range(TT):
                            if i == 8 and tt == 1:
                                pe.wait_ge(y_ready, 12 * l + 10)
                                rows_T(FIRST[l, ("yT", 0)][2], xhat, 2)
                            for k in range(4):
                                ins = token_major(proj_bank(p + tt)[:, 0:w], oT_hi[:, b, k, tt * P:(tt + 1) * P],
                                                  oT_lo[:, b, k, tt * P:(tt + 1) * P], wh[:, k, :], wl[:, k, :], k == 0, k == 3)
                        ins.then_inc(w_used, 1)
                    elif name == "yT":
                        hT_banks[i] = (a, a + 1)
                    elif name in ("wo", "gate", "up"):
                        w = WCOLS[i][1] if name == "wo" else FC
                        for tt in range(TT):
                            proj_take(p + tt)
                        for kh in range(2):
                            hT_ready(kh)
                            unit_ready(n + kh)
                            wh, wl = unit(n + kh, "hi", 4, w), unit(n + kh, "lo", 4, w)
                            for tt in range(TT):
                                if step == ("wo", 0) and (kh, tt) == (0, 1):
                                    pe.wait_ge(y_ready, 12 * (l + 1))
                                    rows_T(FIRST[l, ("yT", 1)][2], xhat, 2, 4)
                                for kk in range(4):
                                    k = 4 * kh + kk
                                    ins = token_major(proj_bank(p + tt)[:, 0:w], hT_hi[:, k, tt * P:(tt + 1) * P],
                                                      hT_lo[:, k, tt * P:(tt + 1) * P], wh[:, kk, :], wl[:, kk, :], k == 0, k == KD - 1)
                            ins.then_inc(w_used, 1)
                    elif name == "hT":
                        for tt in range(TT):
                            proj_read(pe, FIRST[l, ("up", i)][1] + tt)
                        for g, (j, m) in enumerate(block_pairs(i)):
                            aux_take(a + g)
                            for b in range(m):
                                for tt in range(TT):
                                    ins = pe.transpose(aux_bank(a + g)[:, b * T + tt * P:b * T + (tt + 1) * P],
                                                       hid[:, tt, (j + b) * P:(j + b + 1) * P], ident[:, :])
                            ins.then_inc(aux_done, 1)
                    elif name == "down":
                        d = FIRST[l, ("down", 0)][1]
                        k0, kn = down_groups(FT)[i]
                        c = min(cc for cc in range(NF) if blocks_done(cc) >= k0 + kn)
                        for g in range(len(block_pairs(c))):
                            aux_read(pe, FIRST[l, ("hT", c)][2] + g)
                        for h in range(2):
                            if i == 0:
                                for tt in range(TT):
                                    proj_take(d + 2 * tt + h)
                            unit_ready(n + h)
                            wh, wl = unit(n + h, "hi", kn, HALF), unit(n + h, "lo", kn, HALF)
                            for tt in range(TT):
                                for kk in range(kn):
                                    k = k0 + kk
                                    ins = token_major(proj_bank(d + 2 * tt + h), hidT_hi[:, k, tt * P:(tt + 1) * P],
                                                      hidT_lo[:, k, tt * P:(tt + 1) * P], wh[:, kk, :], wl[:, kk, :],
                                                      k == 0, k == FT - 1)
                            ins.then_inc(w_used, 1)

            a = ROUTER_AUX
            pe.wait_ge(router_split, 2)
            aux_take(a)
            for kh in range(2):
                hT_ready(kh)
                for k in range(4 * kh, 4 * kh + 4):
                    plain(aux_bank(a)[0:2 * NE, 0:T], r_split[:, k, :], hT_hi[:, k, :], start=k == 0, stop=False)
                    ins = plain(aux_bank(a)[0:NE, 0:T], r_split[:, k, 0:NE], hT_lo[:, k, :], start=False, stop=k == KD - 1)
            ins.then_inc(aux_done, 1)
            aux_read(pe, a)
            aux_take(a + 1)
            for tt in range(TT):
                ins = plain(aux_bank(a + 1)[:, tt * NE:(tt + 1) * NE], lgT[0:2 * NE, tt * P:(tt + 1) * P], fold[0:2 * NE, :])
            ins.then_inc(aux_done, 1)
            a += 1
            pe.wait_ge(picked_ready, 1)
            aux_take(a + 1)
            bank = aux_bank(a + 1)
            plain(bank[:, 0:NE], tri1[:, :], picked[:, 0, :])
            plain(bank[:, NE:2 * NE], tri1[:, :], picked[:, 1, :], stop=False)
            plain(bank[:, NE:2 * NE], ones[:, :], picked[:, 0, :], start=False)
            plain(bank[:, 2 * NE:3 * NE], ones[:, :], picked[:, 0, :], stop=False)
            plain(bank[:, 2 * NE:3 * NE], ones[:, :], picked[:, 1, :], start=False).then_inc(aux_done, 1)

            def gather(a0, rows, i=0):
                for g in range(4):
                    aux_take(a0 + g, i, E_AUX)
                    for kk in range(2):
                        k = 2 * g + kk
                        for tt in range(TT):
                            ins = plain(aux_bank(a0 + g)[:, kk * 2 * P:(kk + 1) * 2 * P], rows[:, tt, k * P:(k + 1) * P],
                                        sel[:, tt, :], start=tt == 0, stop=tt == TT - 1)
                    ins.then_inc(aux_done, 1)

            def scatter(a0, i=0):
                for g in range(4):
                    tt, h = g // 2, g % 2
                    aux_take(a0 + g, i, E_AUX)
                    lhsT = selT[:, tt * P:(tt + 1) * P]
                    plain(aux_bank(a0 + g), lhsT, y_hi[:, h * HALF:(h + 1) * HALF], stop=False)
                    plain(aux_bank(a0 + g), lhsT, y_lo[:, h * HALF:(h + 1) * HALF], start=False).then_inc(aux_done, 1)

            pe.wait_ge(sel_ready, 1)
            pe.wait_ge(h_hi_ready, TT)
            gather(GATHER_AUX, h_hi)
            pe.wait_ge(h_lo_ready, TT)
            gather(GATHER_AUX + 4, h_lo)
            for g in range(8):
                aux_read(pe, GATHER_AUX + g)
            pe.wait_ge(moe_zero, 1)
            pe.wait_ge(route_ready, 1)
            iters = pe.value_load(ids[0:1, 7:8], min_val=NE // 2, max_val=MAXPASS // 2)
            with pe.Fori(0, iters) as i:
                for s in range(2):
                    n0, p0 = UNITS0 + s * E_UNITS, PROJ0 + s * E_PROJ
                    slots_s = slice(s * P, (s + 1) * P)

                    def slab(c):
                        for half in range(2):
                            b = p0 + 2 * c + half
                            proj_take(b, i, 2 * E_PROJ)
                            for kh in range(2):
                                n = n0 + 4 * c + 2 * half + kh
                                unit_ready(n, i)
                                wh, wl = unit(n, "hi", 4, FC), unit(n, "lo", 4, FC)
                                for kk in range(4):
                                    k = 4 * kh + kk
                                    ins = token_major(proj_bank(b)[:, 0:FC], xe_hi[:, k, slots_s], xe_lo[:, k, slots_s],
                                                      wh[:, kk, :], wl[:, kk, :], k == 0, k == KD - 1)
                                ins.then_inc(w_used, 1)

                    def turn(c):
                        a = AUX0 + E_TURN[s][c]
                        b0, b1 = (blocks_done(c - 1) if c else 0), blocks_done(c)
                        w = (b1 - b0) * P
                        proj_read(pe, p0 + 2 * c + 1, i, 2 * E_PROJ)
                        aux_take(a, i, E_AUX)
                        for b in range(b0, b1):
                            ins = pe.transpose(aux_bank(a)[:, (b - b0) * P:(b - b0 + 1) * P], ehid[:, b * P:(b + 1) * P], ident[:, :])
                        if c == 0:
                            for tt in range(TT):
                                ins = pe.transpose(aux_bank(a)[:, w + tt * P:w + (tt + 1) * P], sel[:, tt, slots_s].bitcast(F32), ident[:, :])
                        if c == 1:
                            for tt in range(TT):
                                ins = plain(aux_bank(a)[:, w:w + 1], sel[:, tt, slots_s].bitcast(F32),
                                            comb[:, tt, bass.ds(i * 2 + s, 1)], start=tt == 0, stop=tt == TT - 1)
                        ins.then_inc(aux_done, 1)

                    def down(g):
                        k0, kn = down_groups(FET)[g]
                        for h in range(2):
                            n, b = n0 + 4 * NFE + 2 * g + h, p0 + 2 * NFE + h
                            if g == 0:
                                proj_take(b, i, 2 * E_PROJ)
                            unit_ready(n, i)
                            wh, wl = unit(n, "hi", kn, HALF), unit(n, "lo", kn, HALF)
                            for kk in range(kn):
                                k = k0 + kk
                                ins = token_major(proj_bank(b), ehT_hi[:, k, :], ehT_lo[:, k, :], wh[:, kk, :], wl[:, kk, :],
                                                  k == 0, k == FET - 1)
                            ins.then_inc(w_used, 1)

                    def turned_read(c):
                        aux_read(pe, AUX0 + E_TURN[s][c], i, E_AUX)

                    if s == 0:
                        for g in range(4):
                            aux_read(pe, AUX0 + E_GATHER[1] + g - E_AUX, i, E_AUX)
                    slab(0)
                    for h in range(2):
                        proj_read(pe, p0 - 2 + h, i, 2 * E_PROJ)
                    scatter(AUX0 + E_SCATTER[s], i)
                    slab(1)
                    slab(2)
                    turn(0)
                    turn(1)
                    slab(3)
                    if s == 1:
                        pe.wait_ge(sel_ready, i + 2)
                        gather(AUX0 + E_GATHER[0], h_hi, i)
                    turn(2)
                    turned_read(0)
                    turned_read(1)
                    down(0)
                    turn(3)
                    turned_read(2)
                    down(1)
                    if s == 1:
                        gather(AUX0 + E_GATHER[1], h_lo, i)
                    turned_read(3)
                    down(2)
                    down(3)
            for h in range(2):
                proj_read(pe, PROJ0 - 2 + h, iters, 2 * E_PROJ)
            scatter(AUX0, iters)


_INS = ["x", "norm1_g", "w_in", "swa_sinks", "gla_w_gate", "gla_b_gate", "gla_norm_g", "w_branch_a", "w_branch_b",
        "w_branch_c", "w_o", "norm2_g", "ffn_w_gate", "ffn_w_up", "ffn_w_down", "moe_router", "moe_w_gate",
        "moe_w_up", "moe_w_down", "final_norm_g"]


def kernel(**inputs):
    import numpy as np
    import concourse.bacc as bacc
    from concourse.bass_utils import run_bass_kernel_spmd

    nc = bacc.Bacc("TRN2", target_bir_lowering=False, num_devices=1)
    arrays, tensors = {}, {}
    for name in _INS:
        a = np.ascontiguousarray(inputs[name])
        arrays[f"in_{name}"] = a
        tensors[name] = nc.dram_tensor(f"in_{name}", a.shape, mybir.dt.from_np(a.dtype), kind="ExternalInput").ap()
    tensors["out"] = nc.dram_tensor("out_0", (1, T, D), F32, kind="ExternalOutput").ap()
    build(nc, tensors)
    result = run_bass_kernel_spmd(nc, [arrays], core_ids=[0])
    return result.results[0]["out_0"]
```
